# Optimizing a Trainium2 kernel written in Bass

```python
import jax, jax.numpy as jnp
from jax import lax
import numpy as np

D_MODEL = 2048
BATCH = 1
SEQ = 512
DEPTH = 1
DEC_BATCH = 8
DEC_SEQ = 4
PAST_LEN = 4096
PAGE_SIZE = 128

HEAD_DIM = 128
N_META = 16
H_ATT = D_MODEL // 256
H_CONV = D_MODEL // 512
H_MLSTM = D_MODEL // 512
D_ATT = H_ATT * HEAD_DIM
D_CONV = H_CONV * HEAD_DIM
D_MLSTM = H_MLSTM * HEAD_DIM
D_MIX = D_ATT + D_CONV + D_MLSTM
CONV_WIDTH = 3
D_FF = 4 * D_MODEL
Q_BLOCK = 128
CHUNK = 128
D_IN = 3 * D_ATT + 3 * D_CONV + 4 * D_MLSTM + 2 * H_MLSTM
ALPHA = (2 * DEPTH) ** 0.25
BETA_INIT = (8 * DEPTH) ** -0.25
SB_SCALE = HEAD_DIM ** -0.5
SB_BIAS_INIT = -6.0
MLSTM_K_SCALE = HEAD_DIM ** -0.5
LN_EPS = 1e-5
RMS_EPS = 1e-6

kernel_name = 'hymba_sb_conv_mlstm_step'

def _split_points():
    sizes = [D_ATT] * 3 + [D_CONV] * 3 + [D_MLSTM] * 4 + [H_MLSTM] * 2
    pts, acc = [], 0
    for s in sizes[:-1]:
        acc += s
        pts.append(acc)
    return pts

def _heads(t):
    return t.reshape(t.shape[:-1] + (t.shape[-1] // HEAD_DIM, HEAD_DIM))

def layer_norm(x, g, b):
    xf = x.astype(jnp.float32)
    mu = jnp.mean(xf, axis=-1, keepdims=True)
    var = jnp.mean(jnp.square(xf - mu), axis=-1, keepdims=True)
    return ((xf - mu) * lax.rsqrt(var + LN_EPS) * g + b).astype(x.dtype)

def project(x, w_in, b_i, b_f):
    p = x @ w_in
    qa, ka, va, bc, cc, xc, qm, km, vm, om, im, fm = jnp.split(p, _split_points(), axis=-1)
    ig = (im + b_i).astype(jnp.float32)
    lf = jax.nn.log_sigmoid((fm + b_f).astype(jnp.float32))
    return (_heads(qa), _heads(ka), _heads(va), bc, cc * xc,
            _heads(qm), _heads(km) * MLSTM_K_SCALE, _heads(vm), _heads(jax.nn.sigmoid(om)), ig, lf)

def sb_attend(q, k, v, bias, q_pos, k_pos):
    z = (jnp.einsum('bqhd,bkhd->bhqk', q, k).astype(jnp.float32) * SB_SCALE
         + bias.astype(jnp.float32)[None, :, None, None])
    mask = k_pos[None, :] < q_pos[:, None]
    log_keep = jnp.where(mask, jax.nn.log_sigmoid(-z), 0.0)
    log_pass = lax.cumsum(log_keep, axis=3, reverse=True) - log_keep
    a = jnp.where(mask, jnp.exp(jax.nn.log_sigmoid(z) + log_pass), 0.0)
    return jnp.einsum('bhqk,bkhd->bqhd', a, v.astype(jnp.float32))

def short_conv(u_ext, w):
    t = u_ext.shape[1] - (CONV_WIDTH - 1)
    return sum(w[j] * u_ext[:, j:j + t] for j in range(CONV_WIDTH))

def mlstm_chunk(carry, xs):
    c0, n0, m0 = carry
    q, k, v, ig, lf = xs
    L = q.shape[1]
    cf = jnp.moveaxis(jnp.cumsum(lf, axis=1), 1, 2)
    igt = jnp.moveaxis(ig, 1, 2)
    causal = jnp.arange(L)[:, None] >= jnp.arange(L)[None, :]
    log_d = jnp.where(causal, cf[..., :, None] - cf[..., None, :] + igt[..., None, :], -jnp.inf)
    log_inter = cf + m0[..., None]
    m_t = jnp.maximum(log_inter, jnp.max(log_d, axis=-1))
    w = jnp.exp(log_d - m_t[..., None]) * jnp.einsum('bthd,bshd->bhts', q, k)
    s_inter = jnp.exp(log_inter - m_t)
    num = s_inter[..., None] * jnp.einsum('bhvk,bthk->bhtv', c0, q) + jnp.einsum('bhts,bshv->bhtv', w, v)
    den = s_inter * jnp.einsum('bhk,bthk->bht', n0, q) + jnp.sum(w, axis=-1)
    h = num / jnp.maximum(jnp.abs(den), jnp.exp(-m_t))[..., None]
    cf_last = cf[..., -1]
    log_w = cf_last[..., None] - cf + igt
    m_new = jnp.maximum(cf_last + m0, jnp.max(log_w, axis=-1))
    wk = jnp.exp(log_w - m_new[..., None])
    decay = jnp.exp(cf_last + m0 - m_new)
    c_new = decay[..., None, None] * c0 + jnp.einsum('bhs,bshv,bshk->bhvk', wk, v, k)
    n_new = decay[..., None] * n0 + jnp.einsum('bhs,bshk->bhk', wk, k)
    return (c_new, n_new, m_new), jnp.moveaxis(h, 1, 2)

def mlstm_prompt(q, k, v, ig, lf):
    b = q.shape[0]
    n_seq = q.shape[1] - N_META
    f32 = jnp.float32
    ins = (q.astype(f32), k.astype(f32), v.astype(f32), ig, lf)
    st = (jnp.zeros((b, H_MLSTM, HEAD_DIM, HEAD_DIM), f32),
          jnp.zeros((b, H_MLSTM, HEAD_DIM), f32),
          jnp.zeros((b, H_MLSTM), f32))
    st, h_meta = mlstm_chunk(st, tuple(t[:, :N_META] for t in ins))

    def to_chunks(t):
        t = t[:, N_META:]
        return jnp.moveaxis(t.reshape((b, n_seq // CHUNK, CHUNK) + t.shape[2:]), 1, 0)

    st, h_real = lax.scan(mlstm_chunk, st, tuple(to_chunks(t) for t in ins))
    h_real = jnp.moveaxis(h_real, 0, 1).reshape((b, n_seq) + h_real.shape[3:])
    return jnp.concatenate([h_meta, h_real], axis=1), st

def merge_and_mlp(x, h_att, y_conv, h_ml, g_mix, w_out, ln1_g, ln1_b, w_up, w_down, ln2_g, ln2_b):
    b, t = x.shape[:2]
    f32 = jnp.float32
    h = jnp.concatenate([h_att.astype(f32), y_conv.astype(f32).reshape(b, t, H_CONV, HEAD_DIM),
                         h_ml.astype(f32)], axis=2)
    h = h * lax.rsqrt(jnp.mean(h * h, axis=-1, keepdims=True) + RMS_EPS)
    h = (h.reshape(b, t, D_MIX) * g_mix).astype(x.dtype)
    x = layer_norm(ALPHA * x + h @ w_out, ln1_g, ln1_b)
    u = jax.nn.relu(x @ w_up)
    return layer_norm(ALPHA * x + (u * u) @ w_down, ln2_g, ln2_b)

def setup_inputs(seed: int = 0) -> dict:
    key = jax.random.key(seed)
    ks = jax.random.split(key, 23)
    f32 = jnp.float32
    n_pages = PAST_LEN // PAGE_SIZE
    n_phys = (DEC_BATCH * n_pages * 5) // 4

    def nrm(k, shape, scale=1.0):
        return jax.random.normal(k, shape, f32) * scale

    page_table = jax.random.permutation(ks[4], n_phys)[: DEC_BATCH * n_pages]
    page_table = page_table.reshape(DEC_BATCH, n_pages).astype(jnp.int32)
    return {
        'x_prompt': nrm(ks[0], (BATCH, SEQ, D_MODEL)),
        'x_sample': nrm(ks[1], (DEC_BATCH, DEC_SEQ, D_MODEL)),
        'cache_k': nrm(ks[2], (DEPTH, n_phys, PAGE_SIZE, H_ATT, HEAD_DIM)),
        'cache_v': nrm(ks[3], (DEPTH, n_phys, PAGE_SIZE, H_ATT, HEAD_DIM)),
        'page_table': page_table,
        'state_conv': nrm(ks[5], (DEPTH, DEC_BATCH, CONV_WIDTH - 1, D_CONV)),
        'state_C': nrm(ks[6], (DEPTH, DEC_BATCH, H_MLSTM, HEAD_DIM, HEAD_DIM), 0.1),
        'state_n': nrm(ks[7], (DEPTH, DEC_BATCH, H_MLSTM, HEAD_DIM), 0.1),
        'state_m': nrm(ks[8], (DEPTH, DEC_BATCH, H_MLSTM)),
        'meta_tokens': nrm(ks[9], (N_META, D_MODEL)),
        'w_in': nrm(ks[10], (DEPTH, D_MODEL, D_IN), D_MODEL ** -0.5),
        'sb_bias': SB_BIAS_INIT + nrm(ks[22], (DEPTH, H_ATT), 0.1),
        'conv_w': nrm(ks[11], (DEPTH, CONV_WIDTH, D_CONV), CONV_WIDTH ** -0.5),
        'b_i': nrm(ks[12], (DEPTH, H_MLSTM), 0.1),
        'b_f': 3.0 + nrm(ks[13], (DEPTH, H_MLSTM), 0.5),
        'g_mix': 1.0 + nrm(ks[14], (DEPTH, D_MIX), 0.05),
        'w_out': nrm(ks[15], (DEPTH, D_MIX, D_MODEL), BETA_INIT * D_MIX ** -0.5),
        'ln1_g': 1.0 + nrm(ks[16], (DEPTH, D_MODEL), 0.05),
        'ln1_b': nrm(ks[17], (DEPTH, D_MODEL), 0.02),
        'w_up': nrm(ks[18], (DEPTH, D_MODEL, D_FF), D_MODEL ** -0.5),
        'w_down': nrm(ks[19], (DEPTH, D_FF, D_MODEL), BETA_INIT * D_FF ** -0.5),
        'ln2_g': 1.0 + nrm(ks[20], (DEPTH, D_MODEL), 0.05),
        'ln2_b': nrm(ks[21], (DEPTH, D_MODEL), 0.02),
    }

def reference(x_prompt, x_sample, cache_k, cache_v, page_table, state_conv, state_C, state_n, state_m,
              meta_tokens, w_in, sb_bias, conv_w, b_i, b_f, g_mix, w_out, ln1_g, ln1_b, w_up, w_down,
              ln2_g, ln2_b):
    f32 = jnp.float32
    bp, n_seq = x_prompt.shape[0], x_prompt.shape[1]
    bs, n_dec = x_sample.shape[0], x_sample.shape[1]
    t_p = N_META + n_seq
    past = page_table.shape[1] * PAGE_SIZE
    xp = jnp.concatenate([jnp.broadcast_to(meta_tokens[None].astype(x_prompt.dtype), (bp, N_META, D_MODEL)),
                          x_prompt], axis=1)
    xs = x_sample
    k_pos_p = jnp.arange(t_p)
    q_pos_meta = jnp.arange(N_META)
    q_pos_blocks = (N_META + jnp.arange(n_seq)).reshape(n_seq // Q_BLOCK, Q_BLOCK)
    k_pos_s = jnp.arange(past + n_dec)
    q_pos_s = past + jnp.arange(n_dec)

    kp_l, vp_l, cp_l, Cp_l, np_l, mp_l = [], [], [], [], [], []
    ks_l, vs_l, cs_l, Cs_l, ns_l, ms_l = [], [], [], [], [], []
    for l in range(DEPTH):
        qa, ka, va, bc, u, qm, km, vm, om, ig, lf = project(xp, w_in[l], b_i[l], b_f[l])
        bias_l = sb_bias[l]
        att_meta = sb_attend(qa[:, :N_META], ka, va, bias_l, q_pos_meta, k_pos_p)
        q_blocks = jnp.moveaxis(qa[:, N_META:].reshape(bp, n_seq // Q_BLOCK, Q_BLOCK, H_ATT, HEAD_DIM), 1, 0)
        att_blocks = lax.map(lambda qb: sb_attend(qb[0], ka, va, bias_l, qb[1], k_pos_p), (q_blocks, q_pos_blocks))
        att_real = jnp.moveaxis(att_blocks, 0, 1).reshape(bp, n_seq, H_ATT, HEAD_DIM)
        h_att = jnp.concatenate([att_meta, att_real], axis=1)
        u_ext = jnp.concatenate([jnp.zeros((bp, CONV_WIDTH - 1, D_CONV), u.dtype), u], axis=1)
        y_conv = bc * short_conv(u_ext, conv_w[l])
        h_ml, (c_fin, n_fin, m_fin) = mlstm_prompt(qm, km, vm, ig, lf)
        kp_l.append(ka)
        vp_l.append(va)
        cp_l.append(u_ext[:, -(CONV_WIDTH - 1):])
        Cp_l.append(c_fin)
        np_l.append(n_fin)
        mp_l.append(m_fin)
        xp = merge_and_mlp(xp, h_att, y_conv, om * h_ml, g_mix[l], w_out[l],
                           ln1_g[l], ln1_b[l], w_up[l], w_down[l], ln2_g[l], ln2_b[l])

        qa, ka, va, bc, u, qm, km, vm, om, ig, lf = project(xs, w_in[l], b_i[l], b_f[l])
        k_past = cache_k[l][page_table].reshape(bs, past, H_ATT, HEAD_DIM)
        v_past = cache_v[l][page_table].reshape(bs, past, H_ATT, HEAD_DIM)
        k_all = jnp.concatenate([k_past, ka.astype(k_past.dtype)], axis=1)
        v_all = jnp.concatenate([v_past, va.astype(v_past.dtype)], axis=1)
        h_att = sb_attend(qa, k_all, v_all, bias_l, q_pos_s, k_pos_s)
        u_ext = jnp.concatenate([state_conv[l].astype(u.dtype), u], axis=1)
        y_conv = bc * short_conv(u_ext, conv_w[l])
        st0 = (state_C[l].astype(f32), state_n[l].astype(f32), state_m[l].astype(f32))
        (c_s, n_s, m_s), h_ml = mlstm_chunk(st0, (qm.astype(f32), km.astype(f32), vm.astype(f32), ig, lf))
        ks_l.append(ka)
        vs_l.append(va)
        cs_l.append(u_ext[:, -(CONV_WIDTH - 1):])
        Cs_l.append(c_s)
        ns_l.append(n_s)
        ms_l.append(m_s)
        xs = merge_and_mlp(xs, h_att, y_conv, om * h_ml, g_mix[l], w_out[l],
                           ln1_g[l], ln1_b[l], w_up[l], w_down[l], ln2_g[l], ln2_b[l])

    y_prompt = xp[:, N_META:]
    y_sample = xs
    return (y_prompt, y_sample,
            jnp.stack(kp_l), jnp.stack(vp_l), jnp.stack(cp_l), jnp.stack(Cp_l), jnp.stack(np_l), jnp.stack(mp_l),
            jnp.stack(ks_l), jnp.stack(vs_l), jnp.stack(cs_l), jnp.stack(Cs_l), jnp.stack(ns_l), jnp.stack(ms_l))


_drawn_inputs = setup_inputs


def setup_inputs(seed=0):
    import zlib

    import numpy as np

    out = dict(_drawn_inputs(seed))
    spreads = {}
    factors = {'ln1_b': 2.687, 'ln2_b': 2.772}
    for name, (base, spread) in spreads.items():
        noise = np.random.default_rng([zlib.crc32(name.encode()), seed]).standard_normal(out[name].shape)
        drawn = base * np.exp(spread * noise) if base else spread * noise
        out[name] = __import__('jax').numpy.asarray(drawn.astype(out[name].dtype))
    for name, factor in factors.items():
        out[name] = (out[name] * factor).astype(out[name].dtype)
    return out
```

```python
from contextlib import ExitStack

import concourse.bass as bass
from concourse import mybir

F32 = mybir.dt.float32
F32R = mybir.dt.float32r
I32 = mybir.dt.int32
ALU = mybir.AluOpType
ACT = mybir.ActivationFunctionType

P = 128
D = 2048
KT = D // P
NMETA, SEQ = 16, 512
TP = NMETA + SEQ
NB, NQ = 8, 4
NS = NB * NQ
T = TP + NS
HALF = T // 2
NTT = 5
TAIL = T - 4 * P
TT = [(t * P, P if t < 4 else TAIL) for t in range(NTT)]
HA, HC, HM = 8, 4, 4
HD = 128
NPAGE, PAGE = 32, 128
DFF = 4 * D
SCALE = HD ** -0.5
ALPHA = 2 ** 0.25
RMS_EPS, LN_EPS = 1e-6, 1e-5
LOW = -1e30

U_ATT, U_CONV, U_ML = 1, 1 + 3 * HA, 1 + 3 * HA + 3 * HC
COL_CONV = 3 * HA * HD
COL_ML = COL_CONV + 3 * HC * HD
COL_GATE = COL_ML + 4 * HM * HD


class Chain:

    def __init__(self, eng, sem, base=0):
        self.eng, self.sem, self.base, self.n = eng, sem, base, 0

    def __call__(self, ins):
        self.n += 1
        ins.then_inc(self.sem, 1)
        self.eng.wait_ge(self.sem, self.base + self.n)

    def restart(self, base):
        self.base, self.n = base, 0


def flat(ap):
    return ap.rearrange("p a b -> p (a b)")


def two(ap):
    return ap.rearrange("p (a b) -> p a b", a=2)


def page_of(eng, dram, pages, n):
    return bass.ds(eng.value_load(pages[0:1, bass.ds(n, 1)], min_val=0, max_val=dram["cache_k"].shape[1] - 1), 1)


def load_keys(eng, dram, pages, b, s, slot):
    return [eng.dma_start(slot[32 * quarter:32 * (quarter + 1), :, :],
                          dram["cache_k"][0][page_of(eng, dram, pages, b * NPAGE + 8 * quarter + s)]
                          .rearrange("a (r i) h d -> i (a r) (h d)", i=32)) for quarter in range(4)]


def first_keys(raw):
    return raw[:, :, :, :].rearrange("p a k n -> p (a k n)").rearrange("p (r c) -> p r c", r=PAGE // 32)


def every_partition(ap, n):
    return bass.AP(ap.tensor, ap.offset, [[0, P], [1, n]])


def phase_mix(nc, dram, keep):
    ident, ones, hT, qs, tn_dram = keep["ident"], keep["ones"], keep["hT"], keep["qs"], dram["tn_dram"]
    with ExitStack() as ctx:
        def sb(name, shape, dt=F32):
            return ctx.enter_context(nc.sbuf_tensor("mix_" + name, shape, dt))

        def sem(name):
            return ctx.enter_context(nc.semaphore("mix_" + name))

        def ps(name, shape):
            return ctx.enter_context(nc.psum_tensor("mix_" + name, shape, F32))

        xh, xl = sb("xh", [P, KT, T], F32R), sb("xl", [P, KT, T], F32R)
        raw = [keep["raw"][:, i, :, :] for i in range(2)]
        wh = [keep["wh0"], sb("wh1", [P, KT, P], F32R)]
        wl = [keep["wl0"], sb("wl1", [P, KT, P], F32R)]
        prj = [[sb(f"prj{s}{j}", [P, T]) for j in range(3)] for s in range(2)]
        kvn = sb("kvn", [P, 2, NTT, HD])
        prob = [sb(f"prob{i}", [P, T]) for i in range(2)]
        kept = sb("kept", [P, T])
        left = sb("left", [P, T + 1])
        attn = [sb(f"attn{i}", [P, T]) for i in range(2)]
        attnT = sb("attnT", [P, 2, 4, P])
        attnT4 = sb("attnT4", [P, NTT, TAIL])
        mask_lt, mask_le = sb("mask_lt", [P, P]), sb("mask_le", [P, P])
        mask_tail = sb("mask_tail", [TAIL, T])
        mask_tail_le = sb("mask_tail_le", [TAIL, TAIL])
        bias8 = sb("bias8", [P, HA])
        bias_h = [sb(f"bias_h{i}", [P, 1]) for i in range(2)]
        tn = sb("tn", [TAIL, HA])
        rows = sb("rows", [P, T])
        onehot3 = sb("onehot3", [P, HM])
        b_col = sb("b_col", [P, NTT, HM])
        small = sb("small", [HM, 96])
        dec8 = sb("dec8", [NB, HM])
        convw = sb("convw", [P, HC, 3])
        cnew = sb("cnew", [P, 2 + 2 * NB])
        cout = sb("cout", [2 + 2 * NB, HD])
        n0nat = sb("n0nat", [NB, HM, HD])
        n0T = sb("n0T", [P, HM, NB])
        csT = sb("csT", [P, HC, 2 * NB])
        sext = sb("sext", [P, NB * (2 + NQ)])
        qsc = sb("qsc", [P, 2, NS])
        c0 = sb("c0", [P, NB, HD])
        cstate = flat(c0[0:2 * NB, 0:HC, :])
        c0T = attnT[:, :, :, :].rearrange("p a b c -> p (a b) c")
        vw = c0T
        wml, rowsel = (attn[0], prob[1]), attn[1]
        o_raw, o_gate = prj[1][0], prj[1][1]
        cpr, npr, nsm = sb("cpr", [P, HD]), sb("npr", [1, HD]), sb("nsm", [NB, HD])
        ecol = sb("ecol", [P, NTT, 1 + NB])
        sbc = sb("sbc", [P, NS])

        G = [ps(f"G{i}", [P, 2, 512]) for i in range(2)]
        B4, B5 = ps("B4", [P, 512]), ps("B5", [P, 512])
        B67 = ps("B67", [P, 2, 512])
        B6, B7 = B67[:, 0, :], B67[:, 1, :]
        S45 = [B4, B5]

        x_in = [sem(f"x_in{i}") for i in range(2)]
        x_ps, xh_done, xl_done = sem("x_ps"), sem("xh_done"), sem("xl_done")
        raw_full = [sem(f"raw_full{i}") for i in range(2)]
        hi_done, lo_done, unit_done, evac_done = sem("hi_done"), sem("lo_done"), sem("unit_done"), sem("evac_done")
        consts, small_in, masks = sem("consts"), sem("small_in"), sem("masks")
        kvT_done, kv_act, kv_dve = sem("kvT_done"), sem("kv_act"), sem("kv_dve")
        s_done, p_done, a_done, aT_ps, aT_done = (sem(x) for x in ("s_done", "p_done", "a_done", "aT_ps", "aT_done"))
        o_ps, o_free, kv_out = sem("o_ps"), sem("o_free"), sem("kv_out")
        dve, act, pool = sem("dve"), sem("act"), sem("pool")
        (gate_ps, gate_act, gate_dve, cstate_ps, cnew_ps, cnew_done, cout_done, conv_done, conv_out, rowsel_done, rows_ps,
         rows_copied, c0_ps, c0_copied, sml_ps, w_done, qsc_done, num_ps, vwp_done, vws_done, cp_ps, cs_ps, head_done, e_arg,
         e_done, osig_done, kv_free, tn_done, m_out, c0_in, scratch_out, tn_out, bias_done, pages_in, keys_in) = (sem(x) for x in (
             "gate_ps gate_act gate_dve cstate_ps cnew_ps cnew_done cout_done conv_done conv_out rowsel_done rows_ps "
             "rows_copied c0_ps c0_copied sml_ps w_done qsc_done num_ps vwp_done vws_done cp_ps cs_ps head_done e_arg "
             "e_done osig_done kv_free tn_done m_out c0_in scratch_out tn_out bias_done pages_in keys_in").split())
        block = ctx.enter_context(nc.Block())
        NU = 1 + 3 * HA + 3 * HC + 4 * HM
        XT = 4 * NTT
        NSMALL = 6 + HC
        ML_UNITS = (2, 3, 0, 1)
        ML_ORDER = (4, 0, 1, 2, 3)

        @block.sync
        def _(sp):
            w_in = dram["w_in"][0].rearrange("(k p) n -> p k n", p=P)
            meta, xp = dram["meta_tokens"], dram["x_prompt"][0]
            xs = dram["x_sample"].rearrange("b q d -> (b q) d")
            for t, (t0, r) in enumerate(TT):
                if t >= 2:
                    sp.wait_ge(x_ps, 4 * (t - 1))
                x_nat = flat(raw[t % 2][:, :, :])
                if t == 0:
                    sp.dma_start(x_nat[0:NMETA, :], meta).then_inc(x_in[0], 16)
                    sp.dma_start(x_nat[NMETA:P, :], xp[0:P - NMETA, :]).then_inc(x_in[0], 16)
                elif t < 4:
                    sp.dma_start(x_nat[:, :], xp[t0 - NMETA:t0 - NMETA + P, :]).then_inc(x_in[t % 2], 16)
                else:
                    sp.dma_start(x_nat[0:NMETA, :], xp[SEQ - NMETA:SEQ, :]).then_inc(x_in[0], 16)
                    sp.dma_start(x_nat[NMETA:TAIL, :], xs).then_inc(x_in[0], 16)
            sp.wait_ge(x_ps, 4 * NTT)
            sp.dma_start(raw[0][:, :, 0:HM], w_in[:, :, COL_GATE:COL_GATE + HM]).then_inc(raw_full[0], 16)
            sp.dma_start(raw[0][:, :, 32:32 + HM], w_in[:, :, COL_GATE + HM:COL_GATE + 2 * HM]).then_inc(raw_full[0], 16)

            def load(u, parity, col):
                if isinstance(u, int) and u < 2:
                    pass
                else:
                    sp.wait_ge(lo_done, u - 1)
                sp.dma_start(raw[parity][:, :, :], w_in[:, :, col]).then_inc(raw_full[parity], 16)

            for j in range(3):
                load(U_ATT + j, (U_ATT + j) % 2, slice(j * HA * HD, j * HA * HD + HD))
            sp.wait_ge(xh_done, XT)
            sp.wait_ge(xl_done, XT)
            sp.dma_start(dram["x_scratch"][0], xh[:, :, :].bitcast(F32)).then_inc(scratch_out, 16)
            sp.dma_start(dram["x_scratch"][1], xl[:, :, :].bitcast(F32)).then_inc(scratch_out, 16)
            with sp.Fori(0, 3) as i:
                for sub in range(2):
                    for j in range(3):
                        u = U_ATT + 3 + 6 * i + 3 * sub + j
                        h = 1 + 2 * i + sub
                        load(u, (U_ATT + 3 + 3 * sub + j) % 2, bass.ds(j * HA * HD + h * HD, HD))
            for j in range(3):
                u = U_ATT + 3 * (HA - 1) + j
                load(u, u % 2, slice(j * HA * HD + (HA - 1) * HD, (j + 1) * HA * HD))
            for c in range(HC):
                for j in range(3):
                    u = U_CONV + 3 * c + j
                    c0 = COL_CONV + j * HC * HD + c * HD
                    load(u, u % 2, slice(c0, c0 + HD))
            with sp.Fori(0, HM) as m:
                for j, part in enumerate(ML_UNITS):
                    load(U_ML + 4 * m + j, (U_ML + j) % 2, bass.ds(COL_ML + part * HM * HD + m * HD, HD))
            sp.dma_start(keep["pages"][:, :], dram["page_table"].rearrange("(a b) n -> a (b n)", a=1)).then_inc(pages_in, 16)
            sp.wait_ge(pages_in, 16)
            sp.wait_ge(lo_done, NU)
            for load in load_keys(sp, dram, keep["pages"], 0, 0, first_keys(keep["raw"])):
                load.then_inc(keys_in, 16)
            sp.wait_ge(scratch_out, 32)
            sp.wait_ge(keys_in, 64)

        @block.tensor
        def _(pe):
            mm, tr = nc.tensor.matmul, nc.tensor.transpose

            pe.wait_ge(consts, 2)
            for t, (t0, r) in enumerate(TT):
                pe.wait_ge(x_in[t % 2], (32, 16, 48, 32, 80)[t])
                x_nat = flat(raw[t % 2][:, :, :])
                for g in range(4):
                    n = 4 * t + g
                    bank = (B4, B5, B6, B7)[g]
                    if n >= 4:
                        pe.wait_ge(xh_done, n - 3)
                        pe.wait_ge(xl_done, n - 3)
                    for k in range(4):
                        last = tr(bank[:, k * r:(k + 1) * r], x_nat[0:r, (4 * g + k) * P:(4 * g + k + 1) * P],
                                  ident[0:r, 0:r])
                    last.then_inc(x_ps, 1)

            def unit(u, parity, first=False, halves=(0, 1)):
                pe.wait_ge(lo_done, u + 1)
                if not first:
                    pe.wait_ge(evac_done, u - 1)
                for half in halves:
                    cols = slice(half * HALF, (half + 1) * HALF)
                    out = G[parity][:, half, 0:HALF]
                    for k in range(KT):
                        mm(out, wh[parity][:, k, :], xh[:, k, cols], start=(k == 0), stop=False)
                        mm(out, wh[parity][:, k, :], xl[:, k, cols], start=False, stop=False)
                        last = mm(out, wl[parity][:, k, :], xh[:, k, cols], start=False, stop=(k == KT - 1))
                if 1 in halves:
                    last.then_inc(unit_done, 1)

            pe.wait_ge(xh_done, XT)
            pe.wait_ge(xl_done, XT)
            for u in range(4):
                unit(u, u % 2, first=(u < 2))

            pe.wait_ge(gate_dve, 2)
            for t, (t0, r) in enumerate(TT):
                tr(B7[0:r, HM * t:HM * (t + 1)], attn[0][0:HM, t0:t0 + r], ident[0:HM, 0:HM])
            pe.wait_ge(gate_act, 3)
            tr(B7[0:NB, 32:32 + HM], small[0:HM, 64:64 + NB], ident[0:HM, 0:HM]).then_inc(gate_ps, 1)
            pe.wait_ge(gate_dve, 3)

            def kv_transposes(v_T, k_T):
                for t in range(4):
                    tr(B6[:, t * P:(t + 1) * P], v_T[:, t * P:(t + 1) * P], ident[:, :])
                for n, src in enumerate((v_T, k_T)):
                    tr(B7[0:TAIL, n * P:(n + 1) * P], src[:, 4 * P:T], ident[:, :])
                for t in range(4):
                    last = tr(B4[:, t * P:(t + 1) * P], k_T[:, t * P:(t + 1) * P], ident[:, :])
                last.then_inc(kvT_done, 1)

            def scores(q_T, k_T, t):
                if t == 4:
                    for half in range(2):
                        last = mm(S45[half][0:TAIL, 0:HALF], q_T[:, 4 * P:T], k_T[:, half * HALF:(half + 1) * HALF],
                                  start=True, stop=True)
                else:
                    w = (t + 1) * P
                    last = mm(S45[(t + 1) % 2][:, 0:w], q_T[:, t * P:w], k_T[:, 0:w], start=True, stop=True)
                last.then_inc(s_done, 1)

            def attend(h, t, n):
                r = TT[t][1]
                if n > 0:
                    pe.wait_ge(a_done, 5 * h + n + 1)
                    pe.wait_ge(aT_done, 5 * h + n)
                for k in range(t + 1):
                    kr = TT[k][1]
                    last = tr(B6[0:kr, k * r:(k + 1) * r], attn[t % 2][0:r, k * P:k * P + kr], ident[0:r, 0:r])
                last.then_inc(aT_ps, 1)

            def weigh(h, t, n):
                pe.wait_ge(aT_done, 5 * h + n + 1)
                if t == 4:
                    pe.wait_ge(o_free, 2 * h + 2)
                r = TT[t][1]
                out = B7[:, 0:TAIL] if t == 4 else B7[:, t * P:(t + 1) * P]
                for k in range(t + 1):
                    kr = TT[k][1]
                    aT = attnT4[0:kr, k, :] if t == 4 else attnT[0:kr, t % 2, k, :]
                    last = mm(out, kvn[0:kr, 0, k, :], aT, start=(k == 0), stop=(k == t))
                if t in (0, 4):
                    last.then_inc(o_ps, 1)

            def head_slot(h, s, u0):
                q_T, k_T, v_T = prj[s]
                pe.wait_ge(evac_done, 4 + 3 * h)
                pe.wait_ge(o_free, 2 * h + 1)
                kv_transposes(v_T, k_T)
                unit(u0 + 3 * h, (u0 + 3 * s) % 2)
                pe.wait_ge(kv_act, h + 1)
                pe.wait_ge(kv_dve, h + 1)
                scores(q_T, k_T, 4)
                unit(u0 + 3 * h + 1, (u0 + 3 * s + 1) % 2)
                pe.wait_ge(a_done, 5 * h + 1)
                scores(q_T, k_T, 3)
                scores(q_T, k_T, 2)
                attend(h, 4, 0)
                unit(u0 + 3 * h + 2, (u0 + 3 * s + 2) % 2, halves=(0,))
                pe.wait_ge(p_done, 5 * h + 2)
                scores(q_T, k_T, 1)
                pe.wait_ge(p_done, 5 * h + 3)
                scores(q_T, k_T, 0)
                unit(u0 + 3 * h + 2, (u0 + 3 * s + 2) % 2, halves=(1,))
                attend(h, 3, 1)
                attend(h, 2, 2)
                weigh(h, 3, 1)
                attend(h, 1, 3)
                weigh(h, 2, 2)
                attend(h, 0, 4)
                weigh(h, 1, 3)
                weigh(h, 0, 4)
                weigh(h, 4, 0)

            with pe.Fori(0, HA // 2) as i:
                for s in range(2):
                    head_slot(2 * i + s, s, U_ATT + 3)

            for c in range(HC):
                if c == 0:
                    pe.wait_ge(small_in, 16 * NSMALL)
                    pe.wait_ge(o_free, 2 * HA + 1)
                    for cc in range(HC):
                        tr(B7[:, cc * 2 * NB:(cc + 1) * 2 * NB], cstate[:, cc * P:(cc + 1) * P],
                           ident[0:2 * NB, 0:2 * NB])
                    for m in range(HM):
                        last = tr(B7[:, 128 + m * NB:128 + (m + 1) * NB], n0nat[:, m, :], ident[0:NB, 0:NB])
                    last.then_inc(cstate_ps, 1)
                if c < HC - 1:
                    for j in range(3):
                        unit(U_CONV + 3 * (c + 1) + j, (U_CONV + 3 * (c + 1) + j) % 2)
                pe.wait_ge(cnew_done, c + 1)
                if c > 0:
                    pe.wait_ge(cout_done, c)
                tr(B6[0:2 + 2 * NB, 0:P], cnew[:, :], ident[:, :]).then_inc(cnew_ps, 1)
            pe.wait_ge(cout_done, HC)

            def unit_beside(m, j, halves=(0, 1)):
                u = U_ML + 4 * (m + 1) + j
                pe.wait_ge(lo_done, u + 1)
                if j == 0:
                    pe.wait_ge(kv_act, HA + m + 1)
                elif j == 1:
                    pe.wait_ge(c0_copied, m + 1)
                else:
                    pe.wait_ge(evac_done, u)
                parity = (U_ML + j) % 2
                for half in halves:
                    cols = slice(half * HALF, (half + 1) * HALF)
                    out = B67[:, half, 0:HALF]
                    for k in range(KT):
                        mm(out, wh[parity][:, k, :], xh[:, k, cols], start=(k == 0), stop=False)
                        mm(out, wh[parity][:, k, :], xl[:, k, cols], start=False, stop=False)
                        last = mm(out, wl[parity][:, k, :], xh[:, k, cols], start=False, stop=(k == KT - 1))
                if 1 in halves:
                    last.then_inc(unit_done, 1)

            def mlstm_head(m, last_head):
                q_T, k_T, v_T = prj[0]
                pe.wait_ge(evac_done, U_ML + 4 * m + 4)
                kv_transposes(v_T, k_T)
                pe.wait_ge(rowsel_done, m + 1)
                for n, base in enumerate((0, 32)):
                    for half in range(2):
                        mm(G[n][:, half, 0:HALF], ones[base:base + HM, :],
                           rowsel[base:base + HM, half * HALF:(half + 1) * HALF], start=True, stop=True)
                mm(B5[:, 0:NS], ones[64:64 + HM, :], rowsel[64:64 + HM, 0:NS], start=True, stop=True)\
                    .then_inc(rows_ps, 1)
                if not last_head:
                    unit_beside(m, 0)
                pe.wait_ge(kv_dve, HA + m + 1)
                pe.wait_ge(rows_copied, m + 1)

                def gather(n, k):
                    k0, kr = TT[k]
                    w = wml[n % 2]
                    for g, stat in ((0, kvn[0:kr, 0, k, :]), (1, ones[0:kr, :])):
                        if k < 4:
                            mm(G[g][:, 0, k0:512], stat, w[0:kr, k0:512], start=(k == 0), stop=(k == 3))
                        tc = TAIL if k == 4 else NMETA
                        mm(G[g][:, 1, 0:tc], stat, w[0:kr, 512:512 + tc], start=(k == 4), stop=False)

                for n, k in enumerate(ML_ORDER):
                    k0, kr = TT[k]
                    if n > 0:
                        pe.wait_ge(w_done, NTT * m + n)
                    if k < 4:
                        mm(B4[:, k0:512], k_T[:, k0:k0 + P], q_T[:, k0:512], start=True, stop=True)
                        last = mm(B5[:, 0:NMETA], k_T[:, k0:k0 + P], q_T[:, 512:TP], start=True, stop=True)
                    else:
                        last = mm(B5[0:TAIL, 0:TAIL], k_T[:, 512:T], q_T[:, 512:T], start=True, stop=True)
                    last.then_inc(sml_ps, 1)
                    if n == 0:
                        pe.wait_ge(c0_in, 16 * (m + 1))
                        if last_head:
                            pe.wait_ge(kv_act, HA + m + 1)
                        else:
                            pe.wait_ge(evac_done, U_ML + 4 * m + 5)
                        for b in range(NB):
                            tr_last = tr((B6, B7)[b // 4][:, b % 4 * P:(b % 4 + 1) * P], c0[:, b, :], ident[:, :])
                        tr_last.then_inc(c0_ps, 1)
                    else:
                        gather(n - 1, ML_ORDER[n - 1])
                    if n in (1, 3) and not last_head:
                        unit_beside(m, 1, (n // 2,))
                pe.wait_ge(w_done, NTT * (m + 1))
                gather(4, ML_ORDER[4])
                pe.wait_ge(qsc_done, m + 1)
                mm(G[1][:, 1, NMETA:TAIL], ones[:, :], qsc[:, 1, :], start=False, stop=True)
                pe.wait_ge(c0_copied, m + 1)
                for b in range(NB):
                    last = mm(G[0][:, 1, NMETA + NQ * b:NMETA + NQ * (b + 1)], c0T[:, b, :],
                              qsc[:, 0, NQ * b:NQ * (b + 1)], start=False, stop=(b == NB - 1))
                last.then_inc(num_ps, 1)
                if not last_head:
                    unit_beside(m, 2)
                pe.wait_ge(vwp_done, m + 1)
                for k in range(NTT):
                    kr = NMETA if k == 4 else P
                    mm(B4[:, 0:P], vw[0:kr, k, :], kvn[0:kr, 1, k, :], start=(k == 0), stop=(k == 4))
                for k in range(NTT):
                    kr = NMETA if k == 4 else P
                    mm(B5[0:1, 0:P], ecol[0:kr, k, 0:1], kvn[0:kr, 1, k, :], start=(k == 0), stop=(k == 4))
                mm(B5[0:NB, P:2 * P], ecol[0:TAIL, 4, 1:1 + NB], kvn[0:TAIL, 1, 4, :], start=True, stop=True)\
                    .then_inc(cp_ps, 1)
                pe.wait_ge(vws_done, m + 1)
                for b in range(NB):
                    last = mm(G[0][:, b // 4, b % 4 * P:(b % 4 + 1) * P], vw[0:TAIL, b, :], kvn[0:TAIL, 1, 4, :],
                              start=True, stop=True)
                last.then_inc(cs_ps, 1)
                if not last_head:
                    unit_beside(m, 3)
                pe.wait_ge(head_done, m + 1)

            for j in range(4):
                unit(U_ML + j, (U_ML + j) % 2)
            with pe.Fori(0, HM - 1) as m:
                mlstm_head(m, False)
            mlstm_head(HM - 1, True)

        @block.scalar
        def _(ac):
            A = nc.scalar.activation
            step = Chain(ac, act)

            for n in range(XT):
                t, g = divmod(n, 4)
                t0, r = TT[t]
                ac.wait_ge(x_ps, n + 1)
                A(xh[:, 4 * g:4 * g + 4, t0:t0 + r], (B4, B5, B6, B7)[g][:, 0:4 * r].rearrange("p (k r) -> p k r", k=4),
                  ACT.Copy).then_inc(xh_done, 1)

            def split(u, parity, uses, first=False):
                ac.wait_ge(raw_full[parity], uses)
                if not first:
                    ac.wait_ge(unit_done, u - 1)
                A(wh[parity][:, :, :], raw[parity][:, :, :], ACT.Copy).then_inc(hi_done, 1)

            def fills(parity, n):
                return 16 * (n + 1) if parity == 0 else 16 * n

            def evac(u, parity, out, scale=1.0, bank=None):
                ac.wait_ge(unit_done, u + 1)
                A(two(out), (G[parity] if bank is None else bank)[:, :, 0:HALF], ACT.Copy, scale=scale).then_inc(evac_done, 1)

            split(0, 0, fills(0, 1), first=True)
            split(1, 1, fills(1, 1), first=True)
            ac.wait_ge(unit_done, 1)
            A(two(prob[0][0:HM, :]), G[0][0:HM, :, 0:HALF], ACT.Copy).then_inc(gate_act, 1)
            A(two(prob[1][0:HM, :]), G[0][32:32 + HM, :, 0:HALF], ACT.Copy).then_inc(evac_done, 1)
            split(2, 0, fills(0, 2))
            for j in range(3):
                evac(U_ATT + j, (U_ATT + j) % 2, prj[0][j])
                split(3 + j, (3 + j) % 2, fills((3 + j) % 2, (3 + j) // 2 + 1))
            ac.wait_ge(gate_dve, 1)
            step(A(attn[0][0:HM, :], kept[0:HM, :], ACT.Exp))
            A(attn[1][0:HM, :], attn[0][0:HM, :], ACT.Ln, bias=1.0).then_inc(gate_act, 1)
            ac.wait_ge(gate_dve, 2)
            A(rows[32:32 + HM, :], left[0:HM, 0:T], ACT.Exp, scale=-1.0)
            A(rows[64:64 + HM, 0:NS], prob[1][0:HM, 0:NS], ACT.Exp)
            A(small[0:HM, 64:64 + NB], prob[1][0:HM, NQ - 1:NS:NQ], ACT.Exp).then_inc(gate_act, 1)

            def kv_copy(n_before):
                ac.wait_ge(kvT_done, n_before + 1)
                A(kvn[:, 0, 0:4, :], B6[:, :].rearrange("p (t d) -> p t d", t=4), ACT.Copy)
                A(kvn[0:TAIL, :, 4, :], B7[0:TAIL, 0:2 * HD].rearrange("p (n d) -> p n d", n=2), ACT.Copy)\
                    .then_inc(kv_act, 1)

            def sigmoid(h, s, t, n):
                r = TT[t][1]
                w = T if t == 4 else (t + 1) * P
                ac.wait_ge(s_done, 5 * h + n + 1)
                if n >= 2:
                    ac.wait_ge(a_done, 5 * h + n - 1)
                ac.wait_ge(small_in, 16 * NSMALL)
                bias = bias_h[s][0:r, 0:1]
                if t == 4:
                    for half in range(2):
                        ins = A(prob[0][0:r, half * HALF:(half + 1) * HALF], S45[half][0:r, 0:HALF], ACT.Sigmoid,
                                bias=bias, scale=SCALE)
                else:
                    ins = A(prob[n % 2][0:r, 0:w], S45[(t + 1) % 2][0:r, 0:w], ACT.Sigmoid, bias=bias, scale=SCALE)
                ins.then_inc(p_done, 1)

            def copy_aT(h, t, n):
                r = TT[t][1]
                ac.wait_ge(aT_ps, 5 * h + n + 1)
                if t == 4:
                    A(attnT4[:, 0:4, :], B6[:, 0:4 * r].rearrange("p (k r) -> p k r", k=4), ACT.Copy)
                    A(attnT4[0:r, 4, :], B6[0:r, 4 * r:5 * r], ACT.Copy).then_inc(aT_done, 1)
                else:
                    A(attnT[:, t % 2, 0:t + 1, :], B6[:, 0:(t + 1) * P].rearrange("p (k r) -> p k r", k=t + 1),
                      ACT.Copy).then_inc(aT_done, 1)

            ac.wait_ge(small_in, 16 * NSMALL)
            with ac.Fori(0, HA // 2) as i:
                for s in range(2):
                    h = 2 * i + s
                    u0 = U_ATT + 3 + 3 * h
                    q = (U_ATT + 3 + 3 * s) % 2
                    fill0 = (U_ATT + 3 + 3 * s) // 2
                    A(bias_h[s][:, :], bias8[:, bass.ds(h, 1)], ACT.Copy).then_inc(bias_done, 1)
                    ac.wait_ge(kv_free, h + 1)
                    kv_copy(h)
                    A(qs[:, bass.ds(h, 1), :], prj[s][0][:, TP:T].rearrange("p (a n) -> p a n", a=1), ACT.Copy)
                    for j in range(3):
                        if j == 2:
                            sigmoid(h, s, 1, 3)
                            sigmoid(h, s, 0, 4)
                        evac(u0 + j, (q + j) % 2, prj[1 - s][j])
                        if j == 0:
                            split(u0 + 2, q, fills(q, 3 * i + fill0 + 2))
                            ac.wait_ge(bias_done, h + 1)
                            sigmoid(h, s, 4, 0)
                        elif j == 1:
                            split(u0 + 3, 1 - q, fills(1 - q, 3 * i + (U_ATT + 3 + 3 * s + 3) // 2 + 1))
                            sigmoid(h, s, 3, 1)
                            sigmoid(h, s, 2, 2)
                            copy_aT(h, 4, 0)
                        else:
                            for n, t in ((1, 3), (2, 2), (3, 1), (4, 0)):
                                copy_aT(h, t, n)
                            split(u0 + 4, q, fills(q, 3 * i + (U_ATT + 3 + 3 * s + 4) // 2 + 1))

            for c in range(HC):
                if c < HC - 1:
                    if c > 0:
                        ac.wait_ge(conv_done, c)
                    for j in range(3):
                        u = U_CONV + 3 * (c + 1) + j
                        evac(u, u % 2, prj[(c + 1) % 2][j])
                        split(u + 2, u % 2, fills(u % 2, u // 2 + 2))
                ac.wait_ge(cnew_ps, c + 1)
                if c > 0:
                    ac.wait_ge(conv_out, 32 * c)
                A(cout[:, :], B6[0:2 + 2 * NB, 0:HD], ACT.Copy).then_inc(cout_done, 1)
            ac.wait_ge(conv_done, HC)
            ac.wait_ge(kv_free, HA + 1)

            def ml_evac(m, j, bank=None):
                out = (prj[0][2], o_raw, prj[0][0], prj[0][1])[j]
                evac(U_ML + 4 * m + j, (U_ML + j) % 2, out, scale=(SCALE if j == 3 else 1.0), bank=bank)

            def ml_split(m, j):
                split(U_ML + 4 * m + j, (U_ML + j) % 2, fills((U_ML + j) % 2, 2 * m + (U_ML + j) // 2 + 1))

            def mlstm_head(m, last_head):
                kv_copy(HA + m)
                ac.wait_ge(rows_ps, m + 1)
                A(two(prob[0][:, :]), G[0][:, :, 0:HALF], ACT.Copy)
                A(two(kept[:, :]), G[1][:, :, 0:HALF], ACT.Copy)
                A(sbc[:, :], B5[:, 0:NS], ACT.Copy).then_inc(rows_copied, 1)
                if not last_head:
                    ml_split(m + 1, 1)
                ac.wait_ge(evac_done, U_ML + 4 * m + 4)
                A(o_gate[:, :], o_raw[:, :], ACT.Sigmoid).then_inc(osig_done, 1)

                def exp(n):
                    k = ML_ORDER[n]
                    k0, kr = TT[k]
                    ac.wait_ge(e_arg, NTT * m + n + 1)
                    w = wml[n % 2]
                    end = T if k == 4 else TP
                    A(w[0:kr, k0:end], w[0:kr, k0:end], ACT.Exp).then_inc(e_done, 1)

                exp(0)
                exp(1)
                if not last_head:
                    ml_evac(m + 1, 0, B67)
                ac.wait_ge(c0_ps, m + 1)
                for n, bank in enumerate((B6, B7)):
                    ins = A(c0T[:, 4 * n:4 * n + 4, :], bank[:, :].rearrange("p (b v) -> p b v", b=4), ACT.Copy)
                ins.then_inc(c0_copied, 1)
                if not last_head:
                    ml_split(m + 1, 2)
                exp(2)
                exp(3)
                exp(4)
                if not last_head:
                    ac.wait_ge(osig_done, m + 1)
                    ml_evac(m + 1, 1, B67)
                    ml_split(m + 1, 3)
                    ml_evac(m + 1, 2, B67)
                    if not (isinstance(m, int) and m == HM - 2):
                        ml_split(m + 2, 0)
                    ml_evac(m + 1, 3, B67)

            for j in range(4):
                ml_evac(0, j)
                if j < 2:
                    ml_split(0, j + 2)
                elif j == 2:
                    ml_split(1, 0)
            with ac.Fori(0, HM - 2) as m:
                mlstm_head(m, False)
            mlstm_head(HM - 2, False)
            mlstm_head(HM - 1, True)

        @block.vector
        def _(dv):
            V = nc.vector
            step = Chain(dv, dve)

            for n in range(XT):
                t, g = divmod(n, 4)
                t0, r = TT[t]
                dv.wait_ge(xh_done, n + 1)
                V.tensor_tensor(xl[:, 4 * g:4 * g + 4, t0:t0 + r],
                                (B4, B5, B6, B7)[g][:, 0:4 * r].rearrange("p (k r) -> p k r", k=4),
                                xh[:, 4 * g:4 * g + 4, t0:t0 + r].bitcast(F32), ALU.subtract).then_inc(xl_done, 1)

            def split(u, parity):
                dv.wait_ge(hi_done, u + 1)
                V.tensor_tensor(wl[parity][:, :, :], raw[parity][:, :, :], wh[parity][:, :, :].bitcast(F32),
                                ALU.subtract).then_inc(lo_done, 1)

            split(0, 0)
            split(1, 1)
            for u in range(2, 6):
                split(u, u % 2)

            ig, f, cf, lf, x1, m_run = prob[0], prob[1], kept, attn[0], attn[1], left
            bi, bf, m0, seg_tmp = small[0:HM, 0:1], small[0:HM, 1:2], small[0:HM, 2:2 + NB], small[0:HM, 16:16 + NB]

            def seg(x, q=0):
                return x[0:HM, TP + q:T:NQ]

            g4 = slice(0, HM)
            dv.wait_ge(masks, 1)
            dv.wait_ge(small_in, 16 * NSMALL)
            dv.wait_ge(evac_done, 1)
            V.tensor_scalar(ig[g4, :], ig[g4, :], bi, None, ALU.add)
            step(V.tensor_scalar(f[g4, :], f[g4, :], bf, None, ALU.add))
            V.scalar_tensor_tensor(cf[g4, :], f[g4, :], -1.0, f[g4, :], ALU.mult, ALU.min).then_inc(gate_dve, 1)
            step(V.memset(left[g4, 0:T], 1.0))
            dv.wait_ge(gate_act, 2)
            step(V.scalar_tensor_tensor(lf[g4, :], f[g4, :], 0.0, x1[g4, :], ALU.min, ALU.subtract))
            step(V.memset(seg(left), 0.0))
            step(V.tensor_tensor_scan(cf[g4, :], left[g4, 0:T], lf[g4, :], 0.0, ALU.mult, ALU.add))
            V.tensor_copy(x1[g4, :], ig[g4, :])
            V.tensor_copy(f[g4, :], lf[g4, :])
            step(V.tensor_tensor(seg_tmp, seg(lf), m0, ALU.add))
            V.scalar_tensor_tensor(x1[g4, 0:1], lf[g4, 0:1], 0.0, ig[g4, 0:1], ALU.add, ALU.max)
            V.tensor_tensor(seg(x1), seg_tmp, seg(ig), ALU.max)
            V.memset(f[g4, 0:1], LOW)
            step(V.memset(seg(f), LOW))
            step(V.tensor_tensor_scan(m_run[g4, 0:T], f[g4, :], x1[g4, :], 0.0, ALU.add, ALU.max))
            V.tensor_tensor(lf[g4, :], ig[g4, :], cf[g4, :], ALU.subtract)
            V.tensor_copy(small[g4, 72:73], m_run[g4, TP - 1:TP])
            V.tensor_copy(small[g4, 80:80 + NB], seg(m_run, NQ - 1))
            step(V.tensor_tensor(rows[g4, :], cf[g4, :], m_run[g4, 0:T], ALU.subtract))
            for q in range(NQ):
                ins = V.tensor_tensor(f[g4, q:NS:NQ], seg(rows, q), m0, ALU.add)
            ins.then_inc(gate_dve, 1)
            dv.wait_ge(gate_ps, 1)
            V.tensor_copy(b_col[:, 0:4, :], B7[:, 0:4 * HM].rearrange("p (t m) -> p t m", t=4))
            V.tensor_copy(b_col[0:TAIL, 4, :], B7[0:TAIL, 4 * HM:5 * HM])
            V.tensor_copy(dec8[:, :], B7[0:NB, 32:32 + HM]).then_inc(gate_dve, 1)
            step(V.memset(left[:, 0:1], 1.0))
            dv.sem_inc(o_free, 1)

            def k_copy(n_before):
                dv.wait_ge(kvT_done, n_before + 1)
                V.tensor_copy(kvn[:, 1, 0:4, :], B4[:, :].rearrange("p (t d) -> p t d", t=4)).then_inc(kv_dve, 1)

            def stick(h, t, n):
                r = TT[t][1]
                w = T if t == 4 else (t + 1) * P
                p, a = prob[n % 2][0:r, :], attn[t % 2][0:r, :]
                dv.wait_ge(p_done, 5 * h + n + 1)
                if t == 4:
                    step(V.tensor_tensor(p, p, mask_tail[:, :], ALU.mult))
                else:
                    step(V.tensor_tensor(p[:, w - P:w], p[:, w - P:w], mask_lt[:, :], ALU.mult))
                step(V.tensor_scalar(kept[0:r, 0:w], p[:, 0:w], -1.0, 1.0, ALU.mult, ALU.add))
                newest_first = kept[0:r, 0:w][:, ::-1]
                step(V.tensor_tensor_scan(left[0:r, 1:w + 1], newest_first, newest_first, 1.0, ALU.mult, ALU.bypass))
                if t == 4:
                    V.tensor_copy(tn[:, bass.ds(h, 1)], left[0:r, T:T + 1]).then_inc(tn_done, 1)
                if n >= 2:
                    dv.wait_ge(aT_ps, 5 * h + n - 1)
                V.tensor_tensor(a[:, 0:w], p[:, 0:w], left[0:r, 0:w][:, ::-1], ALU.mult).then_inc(a_done, 1)

            D_SLOT = 15
            base = step.n
            with dv.Fori(0, HA // 2) as i:
                for s in range(2):
                    h = 2 * i + s
                    u0 = U_ATT + 3 + 3 * h
                    q = (U_ATT + 3 + 3 * s) % 2
                    step.restart(D_SLOT * h + base)
                    dv.wait_ge(kv_free, h + 1)
                    k_copy(h)
                    split(u0 + 2, q)
                    stick(h, 4, 0)
                    split(u0 + 3, 1 - q)
                    stick(h, 3, 1)
                    stick(h, 2, 2)
                    stick(h, 1, 3)
                    stick(h, 0, 4)
                    split(u0 + 4, q)
                    assert step.n == D_SLOT
                    dv.wait_ge(o_ps, 2 * h + 1)
                    V.tensor_copy(hT[:, bass.ds(h, 1), 0:512], B7[:, :].rearrange("p (a n) -> p a n", a=1)).then_inc(o_free, 1)
                    dv.wait_ge(o_ps, 2 * h + 2)
                    V.tensor_copy(hT[:, bass.ds(h, 1), 512:T], B7[:, 0:TAIL].rearrange("p (a n) -> p a n", a=1))\
                        .then_inc(o_free, 1)
            step.restart(base + D_SLOT * HA)

            dv.wait_ge(kv_free, HA + 1)
            uext = wml[1]
            us = sext[:, :].rearrange("p (b j) -> p b j", b=NB)
            step(V.memset(uext[:, 0:2], 0.0))
            for c in range(HC):
                bc, cc, xc = prj[c % 2]
                dv.wait_ge(evac_done, U_CONV + 3 * c + 3)
                if c == 0:
                    dv.wait_ge(cstate_ps, 1)
                    V.tensor_copy(csT[:, :, :], B7[:, 0:HC * 2 * NB].rearrange("p (c n) -> p c n", c=HC))
                    step(V.tensor_copy(n0T[:, :, :], B7[:, 128:128 + HM * NB].rearrange("p (m b) -> p m b", m=HM)))
                V.tensor_tensor(uext[:, 2:2 + TP], cc[:, 0:TP], xc[:, 0:TP], ALU.mult)
                V.tensor_copy(us[:, :, 0:2], csT[:, c, :].rearrange("p (b j) -> p b j", b=NB))
                step(V.tensor_tensor(us[:, :, 2:2 + NQ], cc[:, TP:T].rearrange("p (b q) -> p b q", b=NB),
                                     xc[:, TP:T].rearrange("p (b q) -> p b q", b=NB), ALU.mult))
                if c > 0:
                    dv.wait_ge(cnew_ps, c)
                V.tensor_copy(cnew[:, 0:2], uext[:, TP:TP + 2])
                V.tensor_copy(cnew[:, 2:2 + 2 * NB].rearrange("p (b j) -> p b j", b=NB), us[:, :, NQ:NQ + 2])\
                    .then_inc(cnew_done, 1)
                y = prob[0]
                ys = y[:, TP:T].rearrange("p (b q) -> p b q", b=NB)
                for j in range(3):
                    w = convw[:, c, j:j + 1]
                    if j == 0:
                        V.tensor_scalar(y[:, 0:TP], uext[:, 0:TP], w, None, ALU.mult)
                        step(V.tensor_scalar(ys, us[:, :, 0:NQ], w, None, ALU.mult))
                    else:
                        V.scalar_tensor_tensor(y[:, 0:TP], uext[:, j:j + TP], w, y[:, 0:TP], ALU.mult, ALU.add)
                        step(V.scalar_tensor_tensor(ys, us[:, :, j:j + NQ], w, ys, ALU.mult, ALU.add))
                V.tensor_tensor(hT[:, HA + c, :], bc[:, :], y[:, :], ALU.mult).then_inc(conv_done, 1)
                dv.wait_ge(conv_done, c + 1)
                if c < HC - 1:
                    for j in range(3):
                        u = U_CONV + 3 * (c + 1) + j
                        split(u + 2, u % 2)

            def mlstm_head(m, last_head):
                q_T, k_T, v_T = prj[0]
                V.tensor_scalar(rowsel[0:68, :], rows[0:68, :], onehot3[0:68, bass.ds(m, 1)], None, ALU.mult)\
                    .then_inc(rowsel_done, 1)
                k_copy(HA + m)
                dv.wait_ge(rows_copied, m + 1)
                dv.wait_ge(evac_done, U_ML + 4 * m + 3)
                step(V.tensor_tensor(qsc[:, 0, :], q_T[:, TP:T], sbc[:, :], ALU.mult))
                for q in range(NQ):
                    ins = V.tensor_tensor(qsc[:, 1, q:NS:NQ], qsc[:, 0, q:NS:NQ],
                                          n0T[:, bass.ds(m, 1), :].rearrange("p a b -> p (a b)"), ALU.mult)
                ins.then_inc(qsc_done, 1)

                def arg(n):
                    k = ML_ORDER[n]
                    k0, kr = TT[k]
                    end = T if k == 4 else TP
                    if n >= 2:
                        dv.wait_ge(sml_ps, NTT * m + n + 1)
                    V.tensor_scalar(wml[n % 2][0:kr, k0:end], prob[0][0:kr, k0:end],
                                    b_col[0:kr, k, bass.ds(m, 1)], 0.0, ALU.add, ALU.min).then_inc(e_arg, 1)

                arg(0)
                arg(1)
                if not last_head:
                    split(U_ML + 4 * m + 5, (U_ML + 1) % 2)
                for n, k in enumerate(ML_ORDER):
                    k0, kr = TT[k]
                    w = wml[n % 2]
                    dv.wait_ge(e_done, NTT * m + n + 1)
                    if k == 4:
                        step(V.tensor_tensor(w[0:kr, 512:T], w[0:kr, 512:T], mask_tail_le[:, :], ALU.mult))
                        V.tensor_copy(ecol[0:kr, 4, 0:1], w[0:kr, TP - 1:TP])
                        step(V.tensor_copy(ecol[0:kr, 4, 1:1 + NB], w[0:kr, TP + NQ - 1:T:NQ]))
                    else:
                        step(V.tensor_tensor(w[:, k0:k0 + P], w[:, k0:k0 + P], mask_le[:, :], ALU.mult))
                        step(V.tensor_copy(ecol[:, k, 0:1], w[:, TP - 1:TP]))
                    dv.wait_ge(sml_ps, NTT * m + n + 1)
                    if k == 4:
                        ins = V.tensor_tensor(w[0:kr, 512:T], w[0:kr, 512:T], B5[0:kr, 0:TAIL], ALU.mult)
                    else:
                        V.tensor_tensor(w[:, k0:512], w[:, k0:512], B4[:, k0:512], ALU.mult)
                        ins = V.tensor_tensor(w[:, 512:TP], w[:, 512:TP], B5[:, 0:NMETA], ALU.mult)
                    ins.then_inc(w_done, 1)
                    if 1 <= n < NTT - 1:
                        arg(n + 1)
                    if n in (0, 4) and not last_head:
                        split(U_ML + 4 * m + 6 + n // 4, (U_ML + n // 4) % 2)
                dv.wait_ge(num_ps, m + 1)
                for k in range(NTT):
                    kr = NMETA if k == 4 else P
                    ins = V.tensor_scalar(vw[0:kr, k, :], kvn[0:kr, 0, k, :], ecol[0:kr, k, 0:1], None, ALU.mult)
                ins.then_inc(vwp_done, 1)
                x, y = wml
                V.tensor_scalar(y[:, 0:512], G[1][:, 0, :], -1.0, None, ALU.mult)
                step(V.tensor_scalar(y[:, 512:T], G[1][:, 1, 0:TAIL], -1.0, None, ALU.mult))
                V.tensor_tensor(x[:, 0:512], y[:, 0:512], G[1][:, 0, :], ALU.max)
                step(V.tensor_tensor(x[:, 512:T], y[:, 512:T], G[1][:, 1, 0:TAIL], ALU.max))
                step(V.tensor_tensor(x[:, :], x[:, :], kept[:, :], ALU.max))
                step(V.reciprocal(x[:, :], x[:, :]))
                V.tensor_tensor(y[:, 0:512], x[:, 0:512], G[0][:, 0, :], ALU.mult)
                step(V.tensor_tensor(y[:, 512:T], x[:, 512:T], G[0][:, 1, 0:TAIL], ALU.mult))
                dv.wait_ge(osig_done, m + 1)
                V.tensor_tensor(hT[:, bass.ds(HA + HC + m, 1), :].rearrange("p a n -> p (a n)"), y[:, :], o_gate[:, :],
                                ALU.mult)
                dv.wait_ge(cp_ps, m + 1)
                for b in range(NB):
                    ins = V.tensor_scalar(vw[0:TAIL, b, :], kvn[0:TAIL, 0, 4, :], ecol[0:TAIL, 4, 1 + b:2 + b], None, ALU.mult)
                ins.then_inc(vws_done, 1)
                if not last_head and not (isinstance(m, int) and m == HM - 2):
                    split(U_ML + 4 * m + 8, U_ML % 2)
                dv.wait_ge(c0_in, 16 * (m + 1))
                V.tensor_copy(cpr[:, :], B4[:, 0:P])
                V.tensor_copy(npr[:, :], B5[0:1, 0:HD])
                V.scalar_tensor_tensor(nsm[:, :], n0nat[:, bass.ds(m, 1), :].rearrange("b a d -> b (a d)"),
                                       dec8[:, bass.ds(m, 1)], B5[0:NB, P:2 * P], ALU.mult, ALU.add)
                dv.wait_ge(cs_ps, m + 1)
                for b in range(NB):
                    last = NQ * b + NQ - 1
                    ins = V.scalar_tensor_tensor(c0[:, b, :], c0[:, b, :], sbc[:, last:last + 1],
                                                 G[0][:, b // 4, b % 4 * P:(b % 4 + 1) * P], ALU.mult, ALU.add)
                ins.then_inc(head_done, 1)
                assert step.n == D_ML, step.n

            D_ML = 16
            base = step.base + step.n
            for j in (2, 3, 4):
                split(U_ML + j, (U_ML + j) % 2)
            with dv.Fori(0, HM - 2) as m:
                step.restart(base + D_ML * m)
                mlstm_head(m, False)
            for m in (HM - 2, HM - 1):
                step.restart(base + D_ML * m)
                mlstm_head(m, m == HM - 1)

        @block.gpsimd
        def _(po):
            G_ = nc.gpsimd
            step = Chain(po, pool)

            def select(ap, op, base, pattern, fill):
                return G_.affine_select(out=ap, in_=ap, compare_op=op, fill=fill, base=base, pattern=pattern,
                                        channel_multiplier=1)

            step(G_.memset(ident[:, :], 0.0))
            select(ident[:, :], ALU.not_equal, 0, [[-1, P]], 1.0).then_inc(consts, 1)
            G_.memset(ones[:, :], 1.0).then_inc(consts, 1)
            po.dma_start(small[0:HM, 0:1], dram["b_i"][0].rearrange("(m a) -> m a", a=1)).then_inc(small_in, 16)
            po.dma_start(small[0:HM, 1:2], dram["b_f"][0].rearrange("(m a) -> m a", a=1)).then_inc(small_in, 16)
            with nc.allow_non_contiguous_dma("a few hundred words"):
                po.dma_start(small[0:HM, 2:2 + NB], dram["state_m"][0].rearrange("b m -> m b")).then_inc(small_in, 16)
                for c in range(HC):
                    po.dma_start(convw[:, c, :], dram["conv_w"][0, :, c * P:(c + 1) * P].rearrange("j p -> p j"))\
                        .then_inc(small_in, 16)
            po.dma_start(cstate, dram["state_conv"][0].rearrange("b j d -> (b j) d")).then_inc(small_in, 16)
            po.dma_start(n0nat[:, :, :], dram["state_n"][0]).then_inc(small_in, 16)
            po.dma_start(bias8[:, :], every_partition(dram["sb_bias"], HA)).then_inc(small_in, 16)
            step(G_.memset(rows[:, :], 0.0))
            step(G_.memset(onehot3[:, :], 0.0))
            for base in (0, 32, 64):
                step(select(onehot3[:, :], ALU.not_equal, -base, [[-1, HM]], 1.0))
            step(G_.memset(mask_lt[:, :], 1.0))
            step(select(mask_lt[:, :], ALU.is_gt, 0, [[-1, P]], 0.0))
            step(G_.memset(mask_le[:, :], 1.0))
            step(G_.affine_select(out=mask_le[:, :], in_=mask_le[:, :], compare_op=ALU.is_ge, fill=0.0, base=0,
                                  pattern=[[1, P]], channel_multiplier=-1))
            same = mask_tail[:, 512:T].rearrange("p (g j) -> p g j", j=NQ)
            step(G_.memset(mask_tail[:, :], 1.0))
            step(select(same, ALU.is_ge, 0, [[-NQ, TAIL // NQ], [0, NQ]], 0.0))
            step(G_.affine_select(out=same, in_=same, compare_op=ALU.is_ge, fill=0.0, base=NQ - 1,
                                  pattern=[[NQ, TAIL // NQ], [0, NQ]], channel_multiplier=-1))
            step(G_.memset(mask_tail[0:NMETA, 512:TP], 1.0))
            step(G_.tensor_copy(mask_tail_le[:, :], mask_tail[:, 512:T]))
            step(G_.affine_select(out=mask_tail_le[:, :], in_=mask_tail_le[:, :], compare_op=ALU.is_ge, fill=0.0, base=0,
                                  pattern=[[1, TAIL]], channel_multiplier=-1))
            step(select(mask_tail[:, 512:T], ALU.is_gt, 0, [[-1, TAIL]], 0.0))
            step(G_.affine_select(out=mask_tail[:, 0:512], in_=mask_tail[:, 0:512], compare_op=ALU.is_ge, fill=0.0,
                                  base=NMETA - 1, pattern=[[0, 512]], channel_multiplier=-1))
            po.sem_inc(masks, 1)
            po.sem_inc(kv_free, 1)
            po.wait_ge(gate_dve, 3)
            with nc.allow_non_contiguous_dma("36 words"):
                po.dma_start(dram["m_prompt"][0, 0].rearrange("(m a) -> m a", a=1), small[0:HM, 72:73]).then_inc(tn_out, 16)
                po.dma_start(dram["m_sample"][0].rearrange("b m -> m b"), small[0:HM, 80:80 + NB]).then_inc(tn_out, 16)

            with po.Fori(0, HA) as h:
                po.wait_ge(kv_act, h + 1)
                po.wait_ge(kv_dve, h + 1)
                for n, name in ((1, "k"), (0, "v")):
                    prompt, sample = dram[name + "_prompt"][0, 0], dram[name + "_sample"][0]
                    po.dma_start(prompt[0:512, bass.ds(h, 1), :].rearrange("(t p) a d -> p (t a) d", p=P),
                                 kvn[:, n, 0:4, :]).then_inc(kv_out, 16)
                    po.dma_start(prompt[512:TP, bass.ds(h, 1), :].rearrange("p a d -> p (a d)"),
                                 kvn[0:NMETA, n, 4, :]).then_inc(kv_out, 16)
                    po.dma_start(sample[:, :, bass.ds(h, 1), :].rearrange("b q a d -> (b q) (a d)"),
                                 kvn[NMETA:TAIL, n, 4, :]).then_inc(kv_out, 16)
                po.wait_ge(kv_out, 96 * h + 96)
                po.sem_inc(kv_free, 1)
            po.wait_ge(tn_done, HA)
            po.dma_start(tn_dram, tn[NMETA:TAIL, :]).then_inc(tn_out, 16)

            po.wait_ge(cstate_ps, 1)
            po.dma_start(c0[:, :, :], dram["state_C"][0, :, 0].rearrange("b v k -> v b k")).then_inc(c0_in, 16)
            for c in range(HC):
                po.wait_ge(cout_done, c + 1)
                po.dma_start(dram["conv_prompt"][0, 0, :, c * P:(c + 1) * P], cout[0:2, :]).then_inc(conv_out, 16)
                po.dma_start(dram["conv_sample"][0].rearrange("b j d -> (b j) d")[:, c * P:(c + 1) * P],
                             cout[2:2 + 2 * NB, :]).then_inc(conv_out, 16)
            po.wait_ge(conv_out, 32 * HC)

            def results(m):
                po.wait_ge(head_done, m + 1)
                po.dma_start(dram["C_sample"][0, :, bass.ds(m, 1)].rearrange("b a v k -> v (b a) k"), c0[:, :, :])\
                    .then_inc(m_out, 16)
                po.dma_start(dram["C_prompt"][0, 0, bass.ds(m, 1)].rearrange("a v k -> (a v) k"), cpr[:, :]).then_inc(m_out, 16)
                po.dma_start(dram["n_prompt"][0, 0, bass.ds(m, 1), :], npr[:, :]).then_inc(m_out, 16)
                po.dma_start(dram["n_sample"][0, :, bass.ds(m, 1), :].rearrange("b a d -> b (a d)"), nsm[:, :])\
                    .then_inc(m_out, 16)
                po.wait_ge(m_out, 64 * m + 64)

            with po.Fori(0, HM - 1) as m:
                results(m)
                po.dma_start(c0[:, :, :], dram["state_C"][0, :, bass.ds(m + 1, 1)].rearrange("b a v k -> v (b a) k"))\
                    .then_inc(c0_in, 16)
            results(HM - 1)
            po.wait_ge(tn_out, 48)


def phase_decode(nc, dram, keep):
    ident, ones, hT, qs = keep["ident"], keep["ones"], keep["hT"], keep["qs"]
    NJ = HA // 2
    STEPS = 8
    NR = PAGE // 32
    ROW = HA * HD
    with ExitStack() as ctx:
        def sb(name, shape, dt=F32):
            return ctx.enter_context(nc.sbuf_tensor("dec_" + name, shape, dt))

        def sem(name):
            return ctx.enter_context(nc.semaphore("dec_" + name))

        def ps(name, shape):
            return ctx.enter_context(nc.psum_tensor("dec_" + name, shape, F32))

        k_nat = [first_keys(keep["raw"]), sb("k_nat1", [P, NR, ROW])]
        kT = [sb(f"kT{i}", [P, NR, HA, 4, 32]) for i in range(2)]
        v_nat = [sb(f"v_nat{i}", [P, 4, ROW]) for i in range(2)]
        qd = sb("qd", [P, NJ, 2, 4, 32])
        prob, kept = sb("prob", [P, 1024]), sb("kept", [P, 1024])
        left, a = sb("left", [P, 1025]), sb("a", [P, 1024])
        aT = sb("aT", [P, STEPS, NJ, 4, 2 * NQ])
        o_sb = sb("o_sb", [P, 2 * HD])
        pages, g_mix = keep["pages"], keep["g_mix"]
        raw, wh0, wl0 = keep["raw"], keep["wh0"], keep["wl0"]
        brow = sb("brow", [P, 1])
        tnrow = sb("tnrow", [1, NB, HA, NQ])
        mrow = sb("mrow", [1, NJ, 4, 2, NQ])
        bias8 = sb("bias8", [1, HA])
        bias_row = sb("bias_row", [1, NJ, 4, 2, NQ])
        mcol = sb("mcol", [P, 1])

        sq = [sb(f"sq{i}", [P, T]) for i in range(4)]
        sd, rs = sb("sd", [P, T]), sb("rs", [P, T])
        pick = sb("pick", [P, 63])
        spread = sb("spread", [P, KT, P])
        eps = sb("eps", [P, 1])

        R, R2 = ps("R", [P, 2, 512]), ps("R2", [P, 512])
        S = ps("S", [P, 2, 512])
        O = ps("O", [P, 512])
        X6, X7 = ps("X6", [P, 512]), ps("X7", [P, 512])

        k_in = [sem(f"k_in{i}") for i in range(2)]
        v_in = [sem(f"v_in{i}") for i in range(2)]
        w_in = [sem(f"w_in{i}") for i in range(2)]
        (small_in, consts, kt_done, qk_done, av_done, q_done, p_done, t_done, t_ps, m_done, m_ps, a_done, aT_ps, aT_done,
         o_copied, oT_ps, o_added, dve, bias_ps, bias_done, bias_row_done, g_in, w_hi0, w_lo0, qd_zero, q_act, norm_consts, sq_done, sq_ps, sd_done, rs_done,
         bc_ps, hn_done) = (sem(x) for x in (
             "small_in consts kt_done qk_done av_done q_done p_done t_done t_ps m_done m_ps a_done aT_ps aT_done "
             "o_copied oT_ps o_added dve bias_ps bias_done bias_row_done "
             "g_in w_hi0 w_lo0 qd_zero q_act norm_consts sq_done sq_ps sd_done rs_done bc_ps hn_done").split())
        SPREAD = (R[:, 0, :], R[:, 1, :], R2)
        block = ctx.enter_context(nc.Block())

        @block.sync
        def _(sp):
            sp.sem_inc(k_in[0], 64)
            def load_k(b, s):
                if not (isinstance(b, int) and b == 0 and s < 2):
                    sp.wait_ge(kt_done, 8 * b + s - 1)
                for load in load_keys(sp, dram, pages, b, s, k_nat[s % 2]):
                    load.then_inc(k_in[s % 2], 16)

            def load_v(b, s):
                if not (isinstance(b, int) and b == 0 and s < 2):
                    sp.wait_ge(av_done, 8 * b + s - 1)
                for quarter in range(4):
                    src = dram["cache_v"][0][page_of(sp, dram, pages, b * NPAGE + 8 * quarter + s)].rearrange("a t h d -> (a t) (h d)")
                    sp.dma_start(v_nat[s % 2][:, quarter, :], src).then_inc(v_in[s % 2], 16)

            load_k(0, 1)
            sp.dma_start(bias8[:, :], dram["sb_bias"]).then_inc(small_in, 16)
            with nc.allow_non_contiguous_dma("a vector of the width"):
                sp.dma_start(g_mix[:, :], dram["g_mix"][0].rearrange("(k p) -> p k", p=P)).then_inc(g_in, 16)
            with nc.allow_non_contiguous_dma("256 words"):
                for b in range(NB):
                    sp.dma_start(tnrow[:, b, :, :], dram["tn_dram"][NQ * b:NQ * (b + 1), :].rearrange("(a q) h -> a h q", a=1))\
                        .then_inc(small_in, 16)
            for s in range(2, STEPS):
                load_k(0, s)
            load_k(1, 0)
            load_v(0, 0)
            load_k(1, 1)
            load_v(0, 1)
            for s in range(2, STEPS):
                load_k(1, s)
                load_v(0, s)
            with sp.Fori(2, NB) as b:
                for s in range(STEPS):
                    load_k(b, s)
                    load_v(b - 1, s)
            for s in range(STEPS):
                load_v(NB - 1, s)
            sp.wait_ge(kt_done, 8 * NB)
            for u in range(2):
                sp.dma_start(raw[:, u, :, :], dram["w_out"][0][:, u * P:(u + 1) * P].rearrange("(k p) n -> p k n", p=P))\
                    .then_inc(w_in[u], 16)
            sp.wait_ge(w_in[1], 16)

        @block.gpsimd
        def _(po):
            G_ = nc.gpsimd
            G_.memset(eps[:, :], RMS_EPS)
            G_.memset(left[:, 0:1], 1.0).then_inc(consts, 1)
            po.wait_ge(consts, 1)
            po.wait_ge(qd_zero, 1)

            def queries(b, groups=(0, 1)):
                for g in groups:
                    for quarter in range(4):
                        for db in range(4):
                            c = 8 * quarter + NQ * g
                            ins = G_.tensor_copy(qd[32 * quarter:32 * (quarter + 1), :, g, db, c:c + NQ],
                                                 qs[32 * db:32 * (db + 1), g:HA:2, bass.ds(NQ * b, NQ)])
                ins.then_inc(q_done, 1)

            queries(0, (0,))
            po.wait_ge(q_done, 1)
            po.wait_ge(q_act, 1)
            G_.memset(pick[:, :], 0.0).then_inc(norm_consts, 1)
            G_.memset(spread[:, :, :], 0.0).then_inc(norm_consts, 1)
            po.wait_ge(norm_consts, 2)
            G_.memset(pick[:, 31:32], 1.0).then_inc(norm_consts, 1)
            G_.affine_select(out=spread[:, :, :].rearrange("p (i j) c -> p i j c", j=4),
                             in_=spread[:, :, :].rearrange("p (i j) c -> p i j c", j=4), compare_op=ALU.not_equal, fill=1.0,
                             base=0, pattern=[[-1, 4], [-32, 4], [0, P]], channel_multiplier=1).then_inc(norm_consts, 1)
            with po.Fori(1, NB) as b:
                po.wait_ge(qk_done, 8 * b)
                queries(b)

        @block.vector
        def _(dv):
            V = nc.vector
            step = Chain(dv, dve)
            V.memset(qd[:, :, :, :, :], 0.0).then_inc(qd_zero, 1)
            V.memset(O[:, :], 0.0)

            def k_transpose(b, s):
                dv.wait_ge(k_in[s % 2], 64 * (4 * b + s // 2 + 1))
                if not (isinstance(b, int) and b == 0 and s < 2):
                    dv.wait_ge(qk_done, 8 * b + s - 1)
                V.transpose(flat(kT[s % 2][:, :, :, :, :].rearrange("p r h b i -> p r (h b i)")), flat(k_nat[s % 2][:, :, :]))\
                    .then_inc(kt_done, 1)

            def stick(b):
                dv.wait_ge(p_done, b + 1)
                step(V.tensor_scalar(kept[:, :], prob[:, :], -1.0, 1.0, ALU.mult, ALU.add))
                V.tensor_tensor_scan(left[:, 1:1025], kept[:, ::-1], kept[:, ::-1], 1.0, ALU.mult, ALU.bypass)\
                    .then_inc(t_done, 1)
                dv.wait_ge(t_ps, b + 1)
                total = X6[0:1, 0:P].rearrange("a (j w g q) -> a j w g q", j=NJ, w=4, g=2)
                step(V.tensor_copy(mrow[:, :, 3, :, :], tnrow[:, bass.ds(b, 1), :, :].rearrange("a b (j g) q -> a (b j) g q", g=2)))
                for w in (2, 1, 0):
                    ins = V.tensor_tensor(mrow[:, :, w, :, :], mrow[:, :, w + 1, :, :], total[:, :, w + 1, :, :], ALU.mult)
                    if w:
                        step(ins)
                ins.then_inc(m_done, 1)
                dv.wait_ge(m_ps, b + 1)
                step(V.tensor_copy(mcol[:, :], X6[:, P:P + 1]))
                V.scalar_tensor_tensor(a[:, :], prob[:, :], mcol[:, 0:1], left[:, 0:1024][:, ::-1], ALU.mult, ALU.mult)\
                    .then_inc(a_done, 1)
                return

            D_B = 5

            def add_output(b):
                dv.wait_ge(oT_ps, b + 1)
                for g in range(2):
                    src = X7[:, g * P:(g + 1) * P].rearrange("p (j c) -> p j c", j=NJ)[:, :, NQ * g:NQ * (g + 1)]
                    out = hT[:, g:HA:2, bass.ds(TP + NQ * b, NQ)]
                    ins = V.tensor_tensor(out, out, src, ALU.add)
                ins.then_inc(o_added, 1)

            def head_norm(i):
                h, c = divmod(i, 2)
                end = TP if h < HA and c else (c + 1) * HALF
                x = hT[:, h, c * HALF:end]
                dv.wait_ge(bc_ps, i + 1)
                V.scalar_tensor_tensor(x, x, g_mix[:, h:h + 1], SPREAD[i % 3][:, 0:end - c * HALF], ALU.mult, ALU.mult)\
                    .then_inc(hn_done, 1)

            for s in range(STEPS):
                k_transpose(0, s)
                if s == 3:
                    dv.wait_ge(small_in, 16 * (1 + NB))
                    for w in range(4):
                        for q in range(NQ):
                            ins = V.tensor_copy(bias_row[:, :, w, :, q], bias8[:, :].rearrange("a (j g) -> a j g", g=2))
                    ins.then_inc(bias_row_done, 1)
            dv.wait_ge(consts, 1)
            dv.wait_ge(sd_done, 1)
            V.reciprocal(rs[:, :], sd[:, :]).then_inc(rs_done, 1)
            stick(0)
            assert step.n == D_B
            with dv.Fori(1, NB) as b:
                step.restart(D_B * b)
                for s in range(STEPS):
                    k_transpose(b, s)
                add_output(b - 1)
                stick(b)
            dv.wait_ge(g_in, 16)
            for i in range(2 * KT):
                head_norm(i)
            dv.wait_ge(w_hi0, 1)
            V.tensor_tensor(wl0[:, :, :], raw[:, 0, :, :], wh0[:, :, :].bitcast(F32), ALU.subtract).then_inc(w_lo0, 1)
            add_output(NB - 1)

        @block.scalar
        def _(ac):
            A = nc.scalar.activation
            ac.wait_ge(qd_zero, 1)
            for quarter in range(4):
                for db in range(4):
                    c = 8 * quarter + NQ
                    ins = A(qd[32 * quarter:32 * (quarter + 1), :, 1, db, c:c + NQ], qs[32 * db:32 * (db + 1), 1:HA:2, 0:NQ],
                            ACT.Copy)
            ins.then_inc(q_act, 1)

            def probabilities(b):
                ac.wait_ge(qk_done, 8 * b + 8)
                A(prob[:, :].rearrange("p (a n) -> p a n", a=2), S[:, :, :], ACT.Sigmoid, bias=brow[:, 0:1], scale=SCALE)\
                    .then_inc(p_done, 1)
                ac.wait_ge(aT_ps, b + 1)
                for n, x in enumerate((X6, X7)):
                    ins = A(aT[:, 4 * n:4 * n + 4, :, :, :].rearrange("p s j w c -> p (s j w c)"), x[:, :], ACT.Copy)
                ins.then_inc(aT_done, 1)

            def output(b):
                ac.wait_ge(av_done, 8 * b + 8)
                A(o_sb[:, :], O[:, 0:2 * HD], ACT.Copy).then_inc(o_copied, 1)

            ac.wait_ge(consts, 1)
            for h in range(KT):
                if h >= 4:
                    ac.wait_ge(sq_ps, h // 4)
                A(sq[h % 4][:, :], hT[:, h, :], ACT.Square).then_inc(sq_done, 1)
            ac.wait_ge(sq_ps, KT // 4)
            A(two(sd[:, :]), R[:, :, 0:HALF], ACT.Sqrt, scale=1.0 / HD, bias=eps[:, 0:1]).then_inc(sd_done, 1)
            ac.wait_ge(bias_ps, 1)
            A(brow[:, :], X6[:, P:P + 1], ACT.Copy).then_inc(bias_done, 1)
            ac.wait_ge(bias_done, 1)
            probabilities(0)
            with ac.Fori(1, NB) as b:
                output(b - 1)
                probabilities(b)
            ac.wait_ge(w_in[0], 16)
            A(wh0[:, :, :], raw[:, 0, :, :], ACT.Copy).then_inc(w_hi0, 1)
            output(NB - 1)

        @block.tensor
        def _(pe):
            mm, tr = nc.tensor.matmul, nc.tensor.transpose

            def scores(b, s):
                pe.wait_ge(kt_done, 8 * b + s + 1)
                if s == 0:
                    pe.wait_ge(q_done, b + 1)
                    if isinstance(b, int) and b == 0:
                        pe.wait_ge(q_act, 1)
                for g in range(2):
                    for db in range(4):
                        for j in range(NJ):
                            last = mm(S[32 * j:32 * (j + 1), s // 4, (s % 4) * P:(s % 4 + 1) * P], qd[:, j, g, db, :],
                                      kT[s % 2][:, :, 2 * j + g, db, :], start=(g == 0 and db == 0), stop=(g == 1 and db == 3))
                last.then_inc(qk_done, 1)

            def weigh(b, s):
                pe.wait_ge(v_in[s % 2], 64 * (4 * b + s // 2 + 1))
                for quarter in range(4):
                    for j in range(NJ):
                        last = mm(O[32 * j:32 * j + 2 * NQ, 0:2 * HD], aT[:, s, j, quarter, :],
                                  v_nat[s % 2][:, quarter, 2 * HD * j:2 * HD * (j + 1)],
                                  start=(s == 0 and quarter == 0), stop=(s == STEPS - 1 and quarter == 3))
                last.then_inc(av_done, 1)

            def join(b):
                pe.wait_ge(t_done, b + 1)
                mm(X6[0:1, 0:P], left[:, 1024:1025], ident[:, :], start=True, stop=True).then_inc(t_ps, 1)
                pe.wait_ge(m_done, b + 1)
                mm(X6[:, P:P + 1], mrow[:, :, :, :, :].rearrange("a j w g q -> a (j w g q)"), ones[0:1, 0:1], start=True, stop=True)\
                    .then_inc(m_ps, 1)
                pe.wait_ge(a_done, b + 1)
                for s in range(STEPS):
                    last = tr((X6, X7)[s // 4][:, (s % 4) * P:(s % 4 + 1) * P], a[:, s * P:(s + 1) * P], ident[:, :])
                last.then_inc(aT_ps, 1)
                pe.wait_ge(aT_done, b + 1)

            def out_transpose(b):
                pe.wait_ge(o_copied, b + 1)
                for g in range(2):
                    last = tr(X7[:, g * P:(g + 1) * P], o_sb[:, g * HD:(g + 1) * HD], ident[:, :])
                last.then_inc(oT_ps, 1)
                pe.wait_ge(o_added, b + 1)

            for s in range(STEPS):
                scores(0, s)
                if s % 2 == 1:
                    i = s // 2
                    pe.wait_ge(norm_consts, 4)
                    pe.wait_ge(sq_done, 4 * i + 4)
                    for c in range(2):
                        for j in range(4):
                            last = mm(R[32 * j:32 * (j + 1), c, 0:HALF], pick[:, 31 - i:63 - i], sq[j][:, c * HALF:(c + 1) * HALF],
                                      start=(i == 0), stop=(i == 3))
                    last.then_inc(sq_ps, 1)
            pe.wait_ge(bias_row_done, 1)
            mm(X6[:, P:P + 1], bias_row[:, :, :, :, :].rearrange("a j w g q -> a (j w g q)"), ones[0:1, 0:1], start=True, stop=True)\
                .then_inc(bias_ps, 1)
            join(0)
            with pe.Fori(1, NB) as b:
                for s in range(STEPS):
                    scores(b, s)
                    weigh(b - 1, s)
                out_transpose(b - 1)
                join(b)
            pe.wait_ge(rs_done, 1)
            for s in range(STEPS):
                weigh(NB - 1, s)
                for i in range(4 * s, 4 * s + 4):
                    if i >= 3:
                        pe.wait_ge(hn_done, i - 2)
                    mm(SPREAD[i % 3][:, 0:HALF], spread[:, i // 2, :], rs[:, i % 2 * HALF:(i % 2 + 1) * HALF], start=True, stop=True)\
                        .then_inc(bc_ps, 1)
            out_transpose(NB - 1)


def product(mm, out, w_hi, w_lo, x_hi, x_lo, tiles, cols):
    for n, (wk, xk) in enumerate(tiles):
        mm(out, w_hi[wk], x_hi[:, xk, cols], start=(n == 0), stop=False)
        mm(out, w_hi[wk], x_lo[:, xk, cols], start=False, stop=False)
        last = mm(out, w_lo[wk], x_hi[:, xk, cols], start=False, stop=(n == len(tiles) - 1))
    return last


def product_as_ready(pe, mm, ready, tiles, units, x_hi, x_lo):
    for n, k in enumerate(tiles):
        pe.wait_ge(ready, n + 1)
        for G, w_hi, w_lo in units:
            for c in range(2):
                out, cols = G[:, c, 0:HALF], slice(c * HALF, (c + 1) * HALF)
                mm(out, w_hi[:, k, :], x_hi[:, k, cols], start=(n == 0), stop=False)
                mm(out, w_hi[:, k, :], x_lo[:, k, cols], start=False, stop=False)
                last = mm(out, w_lo[:, k, :], x_hi[:, k, cols], start=False, stop=(n == len(tiles) - 1))
    return last


HEADS = [*range(HA, KT), *range(HA)]


def phase_out(nc, dram, keep, big):
    ones, hT = keep["ones"], keep["hT"]
    mh, ml, raw, wh, wl = (big[x] for x in ("mh", "ml", "raw", "wh", "wl"))
    y = hT
    with ExitStack() as ctx:
        def sb(name, shape, dt=F32):
            return ctx.enter_context(nc.sbuf_tensor("out_" + name, shape, dt))

        def sem(name):
            return ctx.enter_context(nc.semaphore("out_" + name))

        xr = [sb(f"xr{i}", [P, 2, T]) for i in range(2)]
        sq = [sb(f"sq{i}", [P, T]) for i in range(4)]
        sq_s, sd_s, rs_s = (sb(x, [P, HA, NS]) for x in ("sq_s", "sd_s", "rs_s"))
        total, shift = sb("total", [P, T]), sb("shift", [P, T])
        rs = sb("rs", [P, T])
        vecs = sb("vecs", [P, 2, KT])
        eps = sb("eps", [P, 2])
        G = big["G"]
        R = G[3]
        raw_full = [sem(f"raw_full{i}") for i in range(2)]
        xr_in = [sem(f"xr_in{i}") for i in range(2)]
        (hi_done, lo_done, unit_done, y_done, consts, small_in, sq_done, sq_ps, sd_done, hn_done,
         hh_done, hl_done, total_done, mean_ps, shift_done, c_done, c2_done, c2_ps, sd1_done, rs1_done, t_done,
         x1_done, x1h_done, x1l_done, pair_done, dve) = (sem(x) for x in (
             "hi_done lo_done unit_done y_done consts small_in sq_done sq_ps sd_done hn_done "
             "hh_done hl_done total_done mean_ps shift_done c_done c2_done c2_ps sd1_done rs1_done t_done "
             "x1_done x1h_done x1l_done pair_done dve").split())
        block = ctx.enter_context(nc.Block())
        HALVES = [slice(0, HALF), slice(HALF, T)]

        @block.sync
        def _(sp):
            w_out = dram["w_out"][0].rearrange("(k p) n -> p k n", p=P)

            def load(u, parity):
                if not (isinstance(u, int) and u < 2):
                    sp.dma_start(raw[parity][:, :, :], w_out[:, :, bass.ds(u * P, P)]).then_inc(raw_full[parity], 16)
                sp.dma_start(xr[parity][:, :, :], dram["x_scratch"][:, :, bass.ds(u, 1), :].rearrange("c p a t -> p (c a) t"))\
                    .then_inc(xr_in[parity], 16)

            for u in range(2):
                sp.sem_inc(raw_full[u], 16)
                load(u, u)
            with nc.allow_non_contiguous_dma("three vectors of the width"):
                for n, name in enumerate(("ln1_g", "ln1_b")):
                    sp.dma_start(vecs[:, n, :], dram[name][0].rearrange("(k p) -> p k", p=P)).then_inc(small_in, 16)
            with sp.Fori(1, KT // 2) as i:
                for s in range(2):
                    u = 2 * i + s
                    sp.wait_ge(lo_done, u - 1)
                    sp.wait_ge(y_done, u - 1)
                    load(u, s)
            w_up = dram["w_up"][0].rearrange("(k p) n -> p k n", p=P)
            for n in range(4):
                sp.wait_ge(lo_done, KT + n - 1)
                sp.dma_start(raw[n % 2][:, :, :], w_up[:, :, n * P:(n + 1) * P]).then_inc(raw_full[n % 2], 16)
            for s in range(2):
                sp.wait_ge(raw_full[s], 16 * (KT // 2 + 2))

        @block.gpsimd
        def _(po):
            G_ = nc.gpsimd
            G_.memset(eps[:, 0:1], RMS_EPS)
            G_.memset(eps[:, 1:2], LN_EPS).then_inc(consts, 1)
            for n in range(KT):
                po.wait_ge(y_done, n + 1)
                if n == 0:
                    ins = G_.tensor_copy(total[:, :], y[:, 0, :])
                else:
                    po.wait_ge(total_done, n)
                    ins = G_.tensor_tensor(total[:, :], total[:, :], y[:, n, :], ALU.add)
                ins.then_inc(total_done, 1)

        @block.tensor
        def _(pe):
            mm = nc.tensor.matmul
            pe.wait_ge(sq_done, 1)
            mm(R[:, 0, 0:HA * NS], ones[:, :], flat(sq_s[:, :, :]), start=True, stop=True).then_inc(sq_ps, 1)

            def unit(u, parity):
                pe.wait_ge(lo_done, u + 1)
                if not (isinstance(u, int) and u < 2):
                    pe.wait_ge(y_done, u - 1)
                for c, cols in enumerate(HALVES):
                    last = product(mm, G[parity][:, c, 0:HALF], [wh[parity][:, k, :] for k in range(KT)],
                                   [wl[parity][:, k, :] for k in range(KT)], mh, ml, [(k, k) for k in range(KT)], cols)
                last.then_inc(unit_done, 1)

            pe.wait_ge(lo_done, 1)
            product_as_ready(pe, mm, hl_done, HEADS, [(G[0], wh[0], wl[0])], mh, ml).then_inc(unit_done, 1)
            unit(1, 1)
            with pe.Fori(1, KT // 2) as i:
                for s in range(2):
                    unit(2 * i + s, s)
            pe.wait_ge(total_done, KT)
            for c, cols in enumerate(HALVES):
                last = mm(R[:, c, 0:HALF], ones[:, :], total[:, cols], start=True, stop=True)
            last.then_inc(mean_ps, 1)
            for n in range(KT // 2):
                pe.wait_ge(pair_done, n + 1)
                for c, cols in enumerate(HALVES):
                    last = mm(G[2][:, c, 0:HALF], ones[:, :], sq[2 * n % 4][:, cols], start=(n == 0), stop=(n == KT // 2 - 1))
                last.then_inc(c2_ps, 1)
            pe.wait_ge(lo_done, KT + 2)
            pe.wait_ge(y_done, KT)
            product_as_ready(pe, mm, x1l_done, range(KT), [(G[i], wh[i], wl[i]) for i in range(2)], mh, ml)

        @block.scalar
        def _(ac):
            A = nc.scalar.activation

            def split(u, parity, fills, first):
                ac.wait_ge(raw_full[parity], 16 * fills)
                if not first:
                    ac.wait_ge(unit_done, u - 1)
                A(wh[parity][:, :, :], raw[parity][:, :, :], ACT.Copy).then_inc(hi_done, 1)

            def high(h):
                A(mh[:, h, :], hT[:, h, :], ACT.Copy).then_inc(hh_done, 1)

            ac.sem_inc(hi_done, 1)
            ac.wait_ge(consts, 1)
            A(sq_s[:, :, :], hT[:, 0:HA, TP:T], ACT.Square).then_inc(sq_done, 1)
            for h in range(HA, HA + 4):
                high(h)
            ac.wait_ge(sq_ps, 1)
            A(flat(sd_s[:, :, :]), R[:, 0, 0:HA * NS], ACT.Sqrt, scale=1.0 / HD, bias=eps[:, 0:1]).then_inc(sd_done, 1)
            for h in range(HA + 4, KT):
                high(h)
            ac.wait_ge(hn_done, 1)
            for h in range(HA):
                high(h)
            split(1, 1, 1, True)
            with ac.Fori(1, KT // 2) as i:
                for s in range(2):
                    split(2 * i + s, s, i + 1, False)
            for s in range(2):
                split(KT + s, s, KT // 2 + 1, False)
            ac.wait_ge(mean_ps, 1)
            A(two(shift[:, :]), R[:, :, 0:HALF], ACT.Copy, scale=-1.0 / D).then_inc(shift_done, 1)
            for k in range(KT):
                ac.wait_ge(c_done, k + 1)
                if k >= 4:
                    ac.wait_ge(c2_ps, k // 2 - 1)
                A(sq[k % 4][:, :], y[:, k, :], ACT.Square).then_inc(c2_done, 1)
            ac.wait_ge(c2_ps, KT // 2)
            A(two(total[:, :]), G[2][:, :, 0:HALF], ACT.Sqrt, scale=1.0 / D, bias=eps[:, 1:2]).then_inc(sd1_done, 1)
            ac.wait_ge(small_in, 32)
            for k in range(KT):
                ac.wait_ge(t_done, k + 1)
                A(y[:, k, :], y[:, k, :], ACT.Identity, scale=vecs[:, 0, k:k + 1], bias=vecs[:, 1, k:k + 1]).then_inc(x1_done, 1)
                ac.wait_ge(x1_done, k + 1)
                A(mh[:, k, :], y[:, k, :], ACT.Copy).then_inc(x1h_done, 1)

        @block.vector
        def _(dv):
            V = nc.vector
            step = Chain(dv, dve)

            def split(u, parity):
                dv.wait_ge(hi_done, u + 1)
                V.tensor_tensor(wl[parity][:, :, :], raw[parity][:, :, :], wh[parity][:, :, :].bitcast(F32), ALU.subtract)\
                    .then_inc(lo_done, 1)

            def low(n):
                dv.wait_ge(hh_done, n + 1)
                V.tensor_tensor(ml[:, HEADS[n], :], hT[:, HEADS[n], :], mh[:, HEADS[n], :].bitcast(F32), ALU.subtract)\
                    .then_inc(hl_done, 1)

            dv.sem_inc(lo_done, 1)
            for n in range(4):
                low(n)
            dv.wait_ge(sd_done, 1)
            step(V.reciprocal(rs_s[:, :, :], sd_s[:, :, :]))
            for h in range(HA):
                ins = V.scalar_tensor_tensor(hT[:, h, TP:T], hT[:, h, TP:T], keep["g_mix"][:, h:h + 1], rs_s[:, h, :],
                                             ALU.mult, ALU.mult)
            ins.then_inc(hn_done, 1)
            for n in range(4, KT):
                low(n)
            split(1, 1)
            dv.wait_ge(hl_done, KT)

            def residual(u, parity, fills):
                dv.wait_ge(xr_in[parity], 16 * fills)
                dv.wait_ge(unit_done, u + 1)
                out = y[:, bass.ds(u, 1), :].rearrange("p a (c n) -> p (a c) n", c=2)
                step(V.scalar_tensor_tensor(out, two(xr[parity][:, 0, :]), ALPHA, G[parity][:, :, 0:HALF], ALU.mult, ALU.add))
                V.scalar_tensor_tensor(out, two(xr[parity][:, 1, :]), ALPHA, out, ALU.mult, ALU.add).then_inc(y_done, 1)

            residual(0, 0, 1)
            split(2, 0)
            residual(1, 1, 1)
            split(3, 1)
            with dv.Fori(1, KT // 2 - 1) as i:
                step.restart(2 * i + 1)
                for s in range(2):
                    residual(2 * i + s, s, i + 1)
                    split(2 * i + s + 2, s)
            step.restart(KT - 1)
            for s in range(2):
                residual(KT - 2 + s, s, KT // 2)
                split(KT + s, s)
            dv.wait_ge(shift_done, 1)
            for k in range(KT + 2):
                if k < KT:
                    V.tensor_tensor(y[:, k, :], y[:, k, :], shift[:, :], ALU.add).then_inc(c_done, 1)
                if k % 2 == 1 and k >= 3:
                    n = k // 2 - 1
                    dv.wait_ge(c2_done, 2 * n + 2)
                    V.tensor_tensor(sq[2 * n % 4][:, :], sq[2 * n % 4][:, :], sq[2 * n % 4 + 1][:, :], ALU.add).then_inc(pair_done, 1)
            dv.wait_ge(sd1_done, 1)
            V.reciprocal(rs[:, :], total[:, :]).then_inc(rs1_done, 1)
            dv.wait_ge(rs1_done, 1)
            for k in range(KT):
                V.tensor_tensor(y[:, k, :], y[:, k, :], rs[:, :], ALU.mult).then_inc(t_done, 1)
                if k >= 2:
                    dv.wait_ge(x1h_done, k - 1)
                    V.tensor_tensor(ml[:, k - 2, :], y[:, k - 2, :], mh[:, k - 2, :].bitcast(F32), ALU.subtract).then_inc(x1l_done, 1)
            for k in (KT - 2, KT - 1):
                dv.wait_ge(x1h_done, k + 1)
                V.tensor_tensor(ml[:, k, :], y[:, k, :], mh[:, k, :].bitcast(F32), ALU.subtract).then_inc(x1l_done, 1)


def phase_ff(nc, dram, keep, big):
    mh, ml, raw, wh, wl = (big[x] for x in ("mh", "ml", "raw", "wh", "wl"))
    y = keep["hT"]
    FB = 4
    NBLK = DFF // (FB * P)
    NCOL = D // (FB * P)
    UB = FB + NCOL
    with ExitStack() as ctx:
        def sem(name):
            return ctx.enter_context(nc.semaphore("ff_" + name))

        uh = [ctx.enter_context(nc.sbuf_tensor(f"ff_uh{i}", [P, FB, T], F32R)) for i in range(2)]
        ul = [ctx.enter_context(nc.sbuf_tensor(f"ff_ul{i}", [P, FB, T], F32R)) for i in range(2)]
        u2 = [ctx.enter_context(nc.sbuf_tensor(f"ff_u2{i}", [P, T], F32)) for i in range(2)]
        G = big["G"]
        raw_full = [sem(f"raw_full{i}") for i in range(2)]
        (hi_done, lo_done, up_ps, relu_done, u2_done, uh_done, ul_done, down_ps, y_done, scaled) = (sem(x) for x in (
            "hi_done lo_done up_ps relu_done u2_done uh_done ul_done down_ps y_done scaled".split()))
        block = ctx.enter_context(nc.Block())
        HALVES = [slice(0, HALF), slice(HALF, T)]

        @block.sync
        def _(sp):
            w_up = dram["w_up"][0].rearrange("(k p) n -> p k n", p=P)
            w_down = dram["w_down"][0].rearrange("(b k p) n -> p (b k) n", p=P, k=FB)

            def wait(u):
                sp.wait_ge(lo_done, u - 1)

            def load_up(u, parity, tile):
                wait(u)
                sp.dma_start(raw[parity][:, :, :], w_up[:, :, bass.ds(tile * P, P)]).then_inc(raw_full[parity], 16)

            def load_down(u, parity, b, n):
                wait(u)
                sp.dma_start(raw[parity][:, :, :].rearrange("p (k n) c -> p k (n c)", k=FB),
                             w_down[:, bass.ds(b * FB, FB), n * FB * P:(n + 1) * FB * P]).then_inc(raw_full[parity], 16)

            with sp.Fori(0, NBLK - 1) as b:
                for j in range(FB):
                    load_up(FB + UB * b + j, j % 2, (b + 1) * FB + j)
                for j in range(NCOL):
                    load_down(FB + UB * b + FB + j, j % 2, b, j)
            for j in range(NCOL):
                load_down(FB + UB * (NBLK - 1) + j, j % 2, NBLK - 1, j)

        @block.gpsimd
        def _(po):
            for k in range(KT):
                nc.gpsimd.tensor_scalar(y[:, k, :], y[:, k, :], ALPHA, None, ALU.mult).then_inc(scaled, 1)

        @block.tensor
        def _(pe):
            mm = nc.tensor.matmul

            def up(u, t, parity, first):
                pe.wait_ge(lo_done, u + 1)
                if not first:
                    pe.wait_ge(relu_done, t - 1)
                for c, cols in enumerate(HALVES):
                    last = product(mm, G[parity][:, c, 0:HALF], [wh[parity][:, k, :] for k in range(KT)],
                                   [wl[parity][:, k, :] for k in range(KT)], mh, ml, [(k, k) for k in range(KT)], cols)
                last.then_inc(up_ps, 1)

            def down(u, b, parity, j, ub, first):
                pe.wait_ge(lo_done, u + 1)
                if j == 0:
                    pe.wait_ge(ul_done, FB * b + FB)
                for n in range(FB):
                    if not (first and j == 0 and n < 2):
                        pe.wait_ge(y_done, KT * b + FB * j + n - 1)
                    w, v = ([x[parity][:, FB * k + n, :] for k in range(FB)] for x in (wh, wl))
                    for c, cols in enumerate(HALVES):
                        last = product(mm, G[2 + n % 2][:, c, 0:HALF], w, v, uh[ub], ul[ub], [(k, k) for k in range(FB)], cols)
                    last.then_inc(down_ps, 1)

            pe.sem_inc(up_ps, 2)
            for j in range(2, FB):
                up(j, j, j % 2, False)

            def body(b, ub, first, last_block):
                u0 = FB + UB * b
                if not last_block:
                    for j in range(FB):
                        up(u0 + j, FB * (b + 1) + j, j % 2, False)
                    u0 = u0 + FB
                for j in range(NCOL):
                    down(u0 + j, b, j % 2, j, ub, first)

            body(0, 0, True, False)
            with pe.Fori(0, (NBLK - 2) // 2) as i:
                for s in range(2):
                    body(2 * i + 1 + s, 1 - s, False, False)
            body(NBLK - 1, 1, False, True)

        @block.scalar
        def _(ac):
            A = nc.scalar.activation

            def split(u, parity, fills=0, downs=None):
                if not (isinstance(fills, int) and fills == 0):
                    ac.wait_ge(raw_full[parity], 16 * fills)
                if downs is not None:
                    ac.wait_ge(down_ps, downs)
                A(wh[parity][:, :, :], raw[parity][:, :, :], ACT.Copy).then_inc(hi_done, 1)

            def relu(t, j, first=False):
                ac.wait_ge(up_ps, t + 1)
                if not first:
                    ac.wait_ge(ul_done, t - 1)
                A(two(u2[j % 2][:, :]), G[j % 2][:, :, 0:HALF], ACT.Relu).then_inc(relu_done, 1)

            def high(t, j, ub):
                ac.wait_ge(u2_done, t + 1)
                A(uh[ub][:, j, :], u2[j % 2][:, :], ACT.Copy).then_inc(uh_done, 1)

            ac.sem_inc(hi_done, 2)
            for j in range(2, FB):
                relu(j - 2, j - 2, True)
                split(j, j % 2)
                high(j - 2, j - 2, 0)

            def ff_block(b, ub, first):
                u0 = FB + UB * b
                f0 = (UB // 2) * b
                for j in range(FB):
                    if j < 2:
                        if first:
                            relu(FB - 2 + j, FB - 2 + j)
                            split(u0 + j, j, f0 + 1)
                            high(FB - 2 + j, FB - 2 + j, 0)
                        else:
                            split(u0 + j, j, f0 + 1, downs=KT * b - FB * (1 - j))
                    else:
                        relu(FB * b + FB + j - 2, j - 2)
                        split(u0 + j, j % 2, f0 + 2)
                        high(FB * b + FB + j - 2, j - 2, 1 - ub)
                for j in range(NCOL):
                    if j < 2:
                        relu(FB * b + 2 * FB - 2 + j, FB - 2 + j)
                        split(u0 + FB + j, j, f0 + 3)
                        high(FB * b + 2 * FB - 2 + j, FB - 2 + j, 1 - ub)
                    else:
                        split(u0 + FB + j, j % 2, f0 + 4, downs=KT * b + FB * (j - 1))

            ff_block(0, 0, True)
            with ac.Fori(0, (NBLK - 2) // 2) as i:
                for s in range(2):
                    ff_block(2 * i + 1 + s, 1 - s, False)
            b = NBLK - 1
            u0, f0 = FB + UB * b, (UB // 2) * b
            for j in range(NCOL):
                split(u0 + j, j % 2, f0 + 1 + j // 2, downs=(KT * b - FB * (1 - j)))

        @block.vector
        def _(dv):
            V = nc.vector

            def split(u, parity):
                dv.wait_ge(hi_done, u + 1)
                V.tensor_tensor(wl[parity][:, :, :], raw[parity][:, :, :], wh[parity][:, :, :].bitcast(F32), ALU.subtract)\
                    .then_inc(lo_done, 1)

            def square(t, j):
                dv.wait_ge(relu_done, t + 1)
                V.tensor_tensor(u2[j % 2][:, :], u2[j % 2][:, :], u2[j % 2][:, :], ALU.mult).then_inc(u2_done, 1)

            def low(t, j, ub):
                dv.wait_ge(uh_done, t + 1)
                V.tensor_tensor(ul[ub][:, j, :], u2[j % 2][:, :], uh[ub][:, j, :].bitcast(F32), ALU.subtract).then_inc(ul_done, 1)

            def add(b, n):
                dv.wait_ge(down_ps, KT * b + n + 1)
                if isinstance(b, int) and b == 0:
                    dv.wait_ge(scaled, n + 1)
                out = two(y[:, n, :])
                V.tensor_tensor(out, out, G[2 + n % 2][:, :, 0:HALF], ALU.add).then_inc(y_done, 1)

            dv.sem_inc(lo_done, 2)
            square(0, 0)
            split(2, 0)
            low(0, 0, 0)
            square(1, 1)
            split(3, 1)
            low(1, 1, 0)

            def ff_block(b, ub, first):
                u0, t0 = FB + UB * b, FB * b + FB
                for j in range(FB):
                    if j < 2 and first:
                        square(FB - 2 + j, FB - 2 + j)
                        split(u0 + j, j)
                        low(FB - 2 + j, FB - 2 + j, 0)
                    elif j < 2:
                        for n in range(FB):
                            add(b - 1, FB * (NCOL - 2 + j) + n)
                        split(u0 + j, j)
                    else:
                        square(t0 + j - 2, j - 2)
                        split(u0 + j, j % 2)
                        low(t0 + j - 2, j - 2, 1 - ub)
                for j in range(NCOL):
                    if j < 2:
                        square(t0 + FB - 2 + j, FB - 2 + j)
                        split(u0 + FB + j, j)
                        low(t0 + FB - 2 + j, FB - 2 + j, 1 - ub)
                    else:
                        for n in range(FB):
                            add(b, FB * (j - 2) + n)
                        split(u0 + FB + j, j % 2)

            ff_block(0, 0, True)
            dv.wait_ge(scaled, KT)
            with dv.Fori(0, (NBLK - 2) // 2) as i:
                for s in range(2):
                    ff_block(2 * i + 1 + s, 1 - s, False)
            b = NBLK - 1
            for j in range(2):
                for n in range(FB):
                    add(b - 1, FB * (NCOL - 2 + j) + n)
                split(FB + UB * b + j, j)
            for j in range(2):
                for n in range(FB):
                    add(b, FB * j + n)
                split(FB + UB * b + 2 + j, j)
            for n in range(2 * FB, KT):
                add(b, n)


def phase_end(nc, dram, keep):
    ident, y = keep["ident"], keep["hT"]
    with ExitStack() as ctx:
        def sb(name, shape):
            return ctx.enter_context(nc.sbuf_tensor("end_" + name, shape, F32))

        def sem(name):
            return ctx.enter_context(nc.semaphore("end_" + name))

        gain, offset = sb("gain", [P, D]), sb("offset", [P, D])
        out = [sb(f"out{i}", [P, D]) for i in range(2)]
        stats = sb("stats", [P, 4, 6])
        mv = sb("mv", [P, 2, 4])
        eps = sb("eps", [P, 1])
        X = [ctx.enter_context(nc.psum_tensor(f"end_X{i}", [P, 4, 512], F32)) for i in range(2)]
        small_in, consts, y_ps, moments, sd_done, scale_done, norm_done, gain_done, out_ready, dve = (sem(x) for x in (
            "small_in consts y_ps moments sd_done scale_done norm_done gain_done out_ready dve".split()))
        stored = [sem(f"stored{i}") for i in range(2)]
        block = ctx.enter_context(nc.Block())

        @block.sync
        def _(sp):
            sp.dma_start(gain[:, :], every_partition(dram["ln2_g"], D)).then_inc(small_in, 16)
            sp.dma_start(offset[:, :], every_partition(dram["ln2_b"], D)).then_inc(small_in, 16)
            yp, ys = dram["y_prompt"][0], dram["y_sample"].rearrange("b q d -> (b q) d")
            for t, (t0, r) in enumerate(TT):
                o = out[t % 2]
                sp.wait_ge(out_ready, t + 1)
                if t == 0:
                    sp.dma_start(yp[0:P - NMETA, :], o[NMETA:P, :]).then_inc(stored[0], 16)
                elif t < 4:
                    sp.dma_start(yp[t0 - NMETA:t0 - NMETA + P, :], o[:, :]).then_inc(stored[t % 2], 16)
                else:
                    sp.dma_start(yp[SEQ - NMETA:SEQ, :], o[0:NMETA, :]).then_inc(stored[0], 16)
                    sp.dma_start(ys, o[NMETA:TAIL, :]).then_inc(stored[0], 16)
            sp.wait_ge(stored[0], 64)
            sp.wait_ge(stored[1], 32)

        @block.tensor
        def _(pe):
            for t, (t0, r) in enumerate(TT):
                if t >= 2:
                    pe.wait_ge(norm_done, t - 1)
                for k in range(KT):
                    last = nc.tensor.transpose(X[t % 2][0:r, k // 4, (k % 4) * P:(k % 4 + 1) * P], y[:, k, t0:t0 + r], ident[:, :])
                last.then_inc(y_ps, 1)

        @block.vector
        def _(dv):
            V = nc.vector
            step = Chain(dv, dve)

            def finish(t):
                r = TT[t][1]
                o = out[t % 2][0:r, :]
                dv.wait_ge(small_in, 32)
                dv.wait_ge(norm_done, t + 1)
                V.tensor_tensor(o, o, gain[0:r, :], ALU.mult).then_inc(gain_done, 1)

            for t, (t0, r) in enumerate(TT):
                s = t % 2
                dv.wait_ge(y_ps, t + 1)
                for k in range(4):
                    ins = V.bn_stats(stats[0:r, k, :], X[s][0:r, k, :])
                step(ins)
                V.bn_aggr(mv[0:r, s, 0:2], stats[0:r, :, :].rearrange("p a b -> p (a b)")).then_inc(moments, 1)
                dv.wait_ge(sd_done, t + 1)
                step(V.reciprocal(mv[0:r, s, 2:3], mv[0:r, s, 2:3]))
                V.scalar_tensor_tensor(mv[0:r, s, 3:4], mv[0:r, s, 0:1], -1.0, mv[0:r, s, 2:3], ALU.mult, ALU.mult)\
                    .then_inc(scale_done, 1)
                if t > 0:
                    finish(t - 1)
            finish(NTT - 1)

        @block.scalar
        def _(ac):
            A = nc.scalar.activation
            ac.wait_ge(consts, 1)
            for t, (t0, r) in enumerate(TT):
                s = t % 2
                ac.wait_ge(moments, t + 1)
                A(mv[0:r, s, 2:3], mv[0:r, s, 1:2], ACT.Sqrt, bias=eps[0:r, 0:1]).then_inc(sd_done, 1)
                ac.wait_ge(scale_done, t + 1)
                if t >= 2:
                    ac.wait_ge(stored[s], 16 * (t // 2))
                A(out[s][0:r, :].rearrange("p (a b) -> p a b", a=4), X[s][0:r, :, :], ACT.Identity,
                  scale=mv[0:r, s, 2:3], bias=mv[0:r, s, 3:4]).then_inc(norm_done, 1)

        @block.gpsimd
        def _(po):
            nc.gpsimd.memset(eps[:, :], LN_EPS).then_inc(consts, 1)
            po.wait_ge(small_in, 32)
            for t, (t0, r) in enumerate(TT):
                o = out[t % 2][0:r, :]
                po.wait_ge(gain_done, t + 1)
                nc.gpsimd.tensor_tensor(o, o, offset[0:r, :], ALU.add).then_inc(out_ready, 1)


def phase_mlp(nc, dram, keep):
    with ExitStack() as ctx:
        big = {n: ctx.enter_context(nc.sbuf_tensor("big_" + n, [P, KT, T], F32R)) for n in ("mh", "ml")}
        big["raw"] = [keep["raw"][:, i, :, :] for i in range(2)]
        big["wh"] = [keep["wh0"], ctx.enter_context(nc.sbuf_tensor("big_wh1", [P, KT, P], F32R))]
        big["wl"] = [keep["wl0"], ctx.enter_context(nc.sbuf_tensor("big_wl1", [P, KT, P], F32R))]
        big["G"] = [ctx.enter_context(nc.psum_tensor(f"big_G{i}", [P, 2, 512], F32)) for i in range(4)]
        phase_out(nc, dram, keep, big)
        phase_ff(nc, dram, keep, big)
    phase_end(nc, dram, keep)


_INS = ["x_prompt", "x_sample", "cache_k", "cache_v", "page_table", "state_conv", "state_C", "state_n", "state_m",
        "meta_tokens", "w_in", "sb_bias", "conv_w", "b_i", "b_f", "g_mix", "w_out", "ln1_g", "ln1_b", "w_up", "w_down",
        "ln2_g", "ln2_b"]
_OUTS = [("y_prompt", (1, SEQ, D)), ("y_sample", (NB, NQ, D)),
         ("k_prompt", (1, 1, TP, HA, HD)), ("v_prompt", (1, 1, TP, HA, HD)), ("conv_prompt", (1, 1, 2, HC * HD)),
         ("C_prompt", (1, 1, HM, HD, HD)), ("n_prompt", (1, 1, HM, HD)), ("m_prompt", (1, 1, HM)),
         ("k_sample", (1, NB, NQ, HA, HD)), ("v_sample", (1, NB, NQ, HA, HD)), ("conv_sample", (1, NB, 2, HC * HD)),
         ("C_sample", (1, NB, HM, HD, HD)), ("n_sample", (1, NB, HM, HD)), ("m_sample", (1, NB, HM))]


def program(nc, dram):
    with ExitStack() as ctx:
        def sb(name, shape, dt=F32):
            return ctx.enter_context(nc.sbuf_tensor(name, shape, dt))

        keep = {
            "ident": sb("ident", [P, P]), "ones": sb("ones", [P, P]),
            "hT": sb("hT", [P, KT, T]),
            "qs": sb("qs", [P, HA, NS]),
            "pages": sb("pages", [1, NB * NPAGE], I32),
            "g_mix": sb("g_mix", [P, KT]),
            "raw": sb("raw", [P, 2, KT, P]),
            "wh0": sb("wh0", [P, KT, P], F32R), "wl0": sb("wl0", [P, KT, P], F32R),
        }
        phase_mix(nc, dram, keep)
        phase_decode(nc, dram, keep)
        phase_mlp(nc, dram, keep)


def kernel(**inputs):
    import numpy as np
    import concourse.bacc as bacc
    from concourse.bass_utils import run_bass_kernel_spmd

    nc = bacc.Bacc("TRN2", target_bir_lowering=False, num_devices=1)
    arrays, dram = {}, {}
    for name in _INS:
        a = np.ascontiguousarray(inputs[name])
        arrays["in_" + name] = a
        dram[name] = nc.dram_tensor("in_" + name, a.shape, mybir.dt.from_np(a.dtype), kind="ExternalInput").ap()
    for name, shape in _OUTS:
        dram[name] = nc.dram_tensor("out_" + name, shape, F32, kind="ExternalOutput").ap()
    dram["x_scratch"] = nc.dram_tensor("x_scratch", (2, P, KT, T), F32, kind="Internal").ap()
    dram["tn_dram"] = nc.dram_tensor("tn_scratch", (NS, HA), F32, kind="Internal").ap()
    program(nc, dram)
    r = run_bass_kernel_spmd(nc, [arrays], core_ids=[0])
    return tuple(r.results[0]["out_" + name] for name, _ in _OUTS)
```
